# Optimizing a Trainium2 kernel written in Bass

```python
import math
import jax, jax.numpy as jnp
from jax import lax
import numpy as np

D_MODEL = 2048
BATCH = 1
SEQ = 256
DEPTH = 2

PE_DIM = 256
ATTN_HEADS = 8
ATTN_HEAD_DIM = 128
ATTN_WIDTH = ATTN_HEADS * ATTN_HEAD_DIM
MOBA_BLOCK = 256
MOBA_TOPK = 3
Q_CHUNK = 128
ROPE_DIM = ATTN_HEAD_DIM // 4
ROPE_THETA = 500000.0
SSD_WIDTH = D_MODEL - ATTN_WIDTH
SSD_HEAD_DIM = 64
SSD_HEADS = SSD_WIDTH // SSD_HEAD_DIM
SSD_GROUPS = 2
SSD_HEADS_PER_GROUP = SSD_HEADS // SSD_GROUPS
SSD_STATE = 128
SSD_CONV = 4
SSD_CHUNK = 256
SSD_CONV_DIM = SSD_WIDTH + 2 * SSD_GROUPS * SSD_STATE
MIX_WIDTH = ATTN_WIDTH + SSD_WIDTH
IN_PROJ_DIM = 3 * ATTN_WIDTH + SSD_WIDTH + SSD_CONV_DIM + SSD_HEADS
D_FF = 5632
FFN_CONV = 3
DEEPNORM_ALPHA = (2 * DEPTH) ** 0.25
DEEPNORM_BETA = (8 * DEPTH) ** -0.25
LN_EPS = 1e-5
RMS_EPS = 1e-6

kernel_name = "hybrid_moba_ssd_convffn_deepnorm"

def layer_norm(x, g, b):
    xf = x.astype(jnp.float32)
    mu = jnp.mean(xf, -1, keepdims=True)
    var = jnp.mean(jnp.square(xf - mu), -1, keepdims=True)
    return ((xf - mu) * lax.rsqrt(var + LN_EPS) * g + b).astype(x.dtype)

def rms_norm(x, g):
    xf = x.astype(jnp.float32)
    return (xf * lax.rsqrt(jnp.mean(xf * xf, -1, keepdims=True) + RMS_EPS) * g).astype(x.dtype)

def causal_depthwise_conv(x, w):
    K = w.shape[0]
    S = x.shape[1]
    xp = jnp.pad(x, ((0, 0), (K - 1, 0), (0, 0)))
    return sum(xp[:, k:k + S] * w[k] for k in range(K))

def partial_rope(t, positions):
    half = ROPE_DIM // 2
    inv_freq = 1.0 / (ROPE_THETA ** (jnp.arange(0, ROPE_DIM, 2, dtype=jnp.float32) / ROPE_DIM))
    ang = positions.astype(jnp.float32)[..., None] * inv_freq
    cos = jnp.cos(ang)[:, :, None, :]
    sin = jnp.sin(ang)[:, :, None, :]
    tf = t.astype(jnp.float32)
    t1, t2, rest = tf[..., :half], tf[..., half:ROPE_DIM], tf[..., ROPE_DIM:]
    out = jnp.concatenate([t1 * cos - t2 * sin, t2 * cos + t1 * sin, rest], -1)
    return out.astype(t.dtype)

def moba_attention(q, k, v):
    B, S, H, Dh = q.shape
    nb = -(-S // MOBA_BLOCK)
    sp = nb * MOBA_BLOCK
    topk = min(MOBA_TOPK, nb)
    scale = Dh ** -0.5
    qh = q.transpose(0, 2, 1, 3)
    pad = ((0, 0), (0, 0), (0, sp - S), (0, 0))
    kb = jnp.pad(k.transpose(0, 2, 1, 3), pad).reshape(B, H, nb, MOBA_BLOCK, Dh)
    vb = jnp.pad(v.transpose(0, 2, 1, 3), pad).reshape(B, H, nb, MOBA_BLOCK, Dh)
    k_mean = jnp.mean(kb.astype(jnp.float32), axis=3)
    q_blk = jnp.arange(S) // MOBA_BLOCK
    gate = jnp.einsum('bhsd,bhnd->bhsn', qh.astype(jnp.float32), k_mean)
    eligible = jnp.arange(nb)[None, :] < q_blk[:, None]
    gate = jnp.where(eligible, gate, -jnp.inf)
    _, sel = lax.top_k(gate, topk)
    valid = jnp.arange(topk)[None, :] < q_blk[:, None]
    bi = jnp.arange(B)[:, None, None, None]
    hi = jnp.arange(H)[None, :, None, None]
    n_chunks = S // Q_CHUNK
    sel_len = topk * MOBA_BLOCK

    def chunk(c):
        q0 = c * Q_CHUNK
        qc = lax.dynamic_slice_in_dim(qh, q0, Q_CHUNK, axis=2)
        sc = lax.dynamic_slice_in_dim(sel, q0, Q_CHUNK, axis=2)
        vc = lax.dynamic_slice_in_dim(valid, q0, Q_CHUNK, axis=0)
        own = q0 // MOBA_BLOCK
        k_own = lax.dynamic_index_in_dim(kb, own, axis=2, keepdims=False)
        v_own = lax.dynamic_index_in_dim(vb, own, axis=2, keepdims=False)
        k_sel = kb[bi, hi, sc]
        v_sel = vb[bi, hi, sc]
        s_sel = jnp.einsum('bhqd,bhqtkd->bhqtk', qc, k_sel).astype(jnp.float32) * scale
        s_sel = jnp.where(vc[None, None, :, :, None], s_sel, -jnp.inf)
        s_own = jnp.einsum('bhqd,bhkd->bhqk', qc, k_own).astype(jnp.float32) * scale
        q_pos = q0 + jnp.arange(Q_CHUNK)
        k_pos = own * MOBA_BLOCK + jnp.arange(MOBA_BLOCK)
        s_own = jnp.where(k_pos[None, :] <= q_pos[:, None], s_own, -jnp.inf)
        scores = jnp.concatenate([s_sel.reshape(B, H, Q_CHUNK, sel_len), s_own], -1)
        probs = jax.nn.softmax(scores, axis=-1).astype(v.dtype)
        p_sel = probs[..., :sel_len].reshape(B, H, Q_CHUNK, topk, MOBA_BLOCK)
        p_own = probs[..., sel_len:]
        return (jnp.einsum('bhqtk,bhqtkd->bhqd', p_sel, v_sel)
                + jnp.einsum('bhqk,bhkd->bhqd', p_own, v_own))

    out = lax.map(chunk, jnp.arange(n_chunks))
    return out.transpose(1, 0, 3, 2, 4).reshape(B, S, H * Dh)

def ssd_mixer(z, xbc, dt_raw, conv_w, conv_b, dt_bias, a_log, d_skip, norm_g):
    B, S, _ = xbc.shape
    G, E, P, N, L = SSD_GROUPS, SSD_HEADS_PER_GROUP, SSD_HEAD_DIM, SSD_STATE, SSD_CHUNK
    xbc = jax.nn.silu(causal_depthwise_conv(xbc, conv_w) + conv_b)
    xs, b_in, c_in = jnp.split(xbc, [SSD_WIDTH, SSD_WIDTH + G * N], axis=-1)
    dt = jax.nn.softplus(dt_raw.astype(jnp.float32) + dt_bias)
    a = -jnp.exp(a_log.astype(jnp.float32))
    nc = -(-S // L)
    sp = nc * L

    def pad_s(t):
        return jnp.pad(t, ((0, 0), (0, sp - S)) + ((0, 0),) * (t.ndim - 2))

    x5 = pad_s(xs).reshape(B, nc, L, G, E, P).astype(jnp.float32)
    dt5 = pad_s(dt).reshape(B, nc, L, G, E)
    bm = pad_s(b_in).reshape(B, nc, L, G, N).astype(jnp.float32)
    cm = pad_s(c_in).reshape(B, nc, L, G, N).astype(jnp.float32)
    xdt = x5 * dt5[..., None]
    a_cs = jnp.cumsum((dt5 * a.reshape(G, E)).transpose(0, 3, 4, 1, 2), axis=-1)
    tril = jnp.tril(jnp.ones((L, L), dtype=bool))
    seg = jnp.exp(jnp.where(tril, a_cs[..., :, None] - a_cs[..., None, :], -jnp.inf))
    cb = jnp.einsum('bclgn,bcsgn->bcgls', cm, bm)
    y_diag = jnp.einsum('bcgls,bgecls,bcsgep->bclgep', cb, seg, xdt)
    decay_states = jnp.exp(a_cs[..., -1:] - a_cs)
    states = jnp.einsum('bclgn,bgecl,bclgep->cbgepn', bm, decay_states, xdt)
    chunk_decay = jnp.exp(a_cs[..., -1]).transpose(3, 0, 1, 2)

    def step(h, inp):
        s_c, d_c = inp
        return d_c[..., None, None] * h + s_c, h

    _, states_in = lax.scan(step, jnp.zeros(states.shape[1:], jnp.float32), (states, chunk_decay))
    y_off = jnp.einsum('bclgn,cbgepn,bgecl->bclgep', cm, states_in, jnp.exp(a_cs))
    y = y_diag + y_off + x5 * d_skip.astype(jnp.float32).reshape(G, E)[:, :, None]
    y = y.reshape(B, sp, SSD_WIDTH)[:, :S]
    yg = (y * jax.nn.silu(z.astype(jnp.float32))).reshape(B, S, G, SSD_WIDTH // G)
    yg = yg * lax.rsqrt(jnp.mean(yg * yg, -1, keepdims=True) + RMS_EPS)
    return (yg.reshape(B, S, SSD_WIDTH) * norm_g).astype(z.dtype)

def conv_ffn(x, w_up, conv_w, conv_b, w_down):
    h = causal_depthwise_conv(x @ w_up, conv_w) + conv_b
    g, u = jnp.split(h, 2, axis=-1)
    return (jax.nn.silu(g) * u) @ w_down

def setup_inputs(seed: int = 0) -> dict:
    key = jax.random.key(seed)
    ks = jax.random.split(key, 24)
    nrm = jax.random.normal
    f32 = jnp.float32
    x = nrm(ks[0], (BATCH, SEQ, D_MODEL), f32)
    p = nrm(ks[1], (DEPTH, BATCH, SEQ, PE_DIM), f32)
    positions = jnp.broadcast_to(jnp.arange(SEQ, dtype=jnp.int32)[None, :], (BATCH, SEQ))
    w_in = nrm(ks[2], (DEPTH, D_MODEL, IN_PROJ_DIM), f32) * D_MODEL ** -0.5
    attn_norm_g = 1.0 + 0.02 * nrm(ks[3], (DEPTH, ATTN_WIDTH), f32)
    ssd_conv_w = nrm(ks[4], (DEPTH, SSD_CONV, SSD_CONV_DIM), f32) * SSD_CONV ** -0.5
    ssd_conv_b = 0.02 * nrm(ks[5], (DEPTH, SSD_CONV_DIM), f32)
    dt0 = jnp.exp(jax.random.uniform(ks[6], (DEPTH, SSD_HEADS), f32, math.log(1e-3), math.log(1e-1)))
    ssd_dt_bias = dt0 + jnp.log(-jnp.expm1(-dt0))
    ssd_a_log = jnp.log(jax.random.uniform(ks[7], (DEPTH, SSD_HEADS), f32, 1.0, 16.0))
    ssd_d = 1.0 + 0.1 * nrm(ks[8], (DEPTH, SSD_HEADS), f32)
    ssd_norm_g = 1.0 + 0.02 * nrm(ks[9], (DEPTH, SSD_WIDTH), f32)
    w_out = nrm(ks[10], (DEPTH, MIX_WIDTH, D_MODEL), f32) * MIX_WIDTH ** -0.5 * DEEPNORM_BETA
    ln1_g = 1.0 + 0.02 * nrm(ks[11], (DEPTH, D_MODEL), f32)
    ln1_b = 0.02 * nrm(ks[12], (DEPTH, D_MODEL), f32)
    w_up = nrm(ks[13], (DEPTH, D_MODEL, 2 * D_FF), f32) * D_MODEL ** -0.5
    ffn_conv_w = nrm(ks[14], (DEPTH, FFN_CONV, 2 * D_FF), f32) * FFN_CONV ** -0.5
    ffn_conv_b = 0.02 * nrm(ks[15], (DEPTH, 2 * D_FF), f32)
    w_down = nrm(ks[16], (DEPTH, D_FF, D_MODEL), f32) * D_FF ** -0.5 * DEEPNORM_BETA
    w_pe_gate = nrm(ks[17], (DEPTH, D_MODEL, D_MODEL), f32) * D_MODEL ** -0.5
    w_pe_proj = nrm(ks[18], (DEPTH, PE_DIM, D_MODEL), f32) * PE_DIM ** -0.5 * DEEPNORM_BETA
    ln2_g = 1.0 + 0.02 * nrm(ks[19], (DEPTH, D_MODEL), f32)
    ln2_b = 0.02 * nrm(ks[20], (DEPTH, D_MODEL), f32)
    return {"x": x, "p": p, "positions": positions, "w_in": w_in, "attn_norm_g": attn_norm_g,
            "ssd_conv_w": ssd_conv_w, "ssd_conv_b": ssd_conv_b, "ssd_dt_bias": ssd_dt_bias,
            "ssd_a_log": ssd_a_log, "ssd_d": ssd_d, "ssd_norm_g": ssd_norm_g, "w_out": w_out,
            "ln1_g": ln1_g, "ln1_b": ln1_b, "w_up": w_up, "ffn_conv_w": ffn_conv_w,
            "ffn_conv_b": ffn_conv_b, "w_down": w_down, "w_pe_gate": w_pe_gate,
            "w_pe_proj": w_pe_proj, "ln2_g": ln2_g, "ln2_b": ln2_b}

def reference(x, p, positions, w_in, attn_norm_g, ssd_conv_w, ssd_conv_b, ssd_dt_bias, ssd_a_log,
              ssd_d, ssd_norm_g, w_out, ln1_g, ln1_b, w_up, ffn_conv_w, ffn_conv_b, w_down,
              w_pe_gate, w_pe_proj, ln2_g, ln2_b):
    B, S, _ = x.shape
    A = ATTN_WIDTH
    splits = [A, 2 * A, 3 * A, 3 * A + SSD_WIDTH, 3 * A + SSD_WIDTH + SSD_CONV_DIM]
    h = x
    for i in range(DEPTH):
        proj = h @ w_in[i]
        q, k, v, z, xbc, dt_raw = jnp.split(proj, splits, axis=-1)
        q = partial_rope(q.reshape(B, S, ATTN_HEADS, ATTN_HEAD_DIM), positions)
        k = partial_rope(k.reshape(B, S, ATTN_HEADS, ATTN_HEAD_DIM), positions)
        v = v.reshape(B, S, ATTN_HEADS, ATTN_HEAD_DIM)
        attn_out = rms_norm(moba_attention(q, k, v), attn_norm_g[i])
        ssd_out = ssd_mixer(z, xbc, dt_raw, ssd_conv_w[i], ssd_conv_b[i], ssd_dt_bias[i],
                            ssd_a_log[i], ssd_d[i], ssd_norm_g[i])
        mix = jnp.concatenate([attn_out, ssd_out], axis=-1) @ w_out[i]
        h = layer_norm(DEEPNORM_ALPHA * h + mix, ln1_g[i], ln1_b[i])
        ffn = conv_ffn(h, w_up[i], ffn_conv_w[i], ffn_conv_b[i], w_down[i])
        ple = (p[i] @ w_pe_proj[i]) * jax.nn.sigmoid(h @ w_pe_gate[i])
        h = layer_norm(DEEPNORM_ALPHA * h + ffn + ple, ln2_g[i], ln2_b[i])
    return h


_drawn_inputs = setup_inputs


def setup_inputs(seed=0):
    import zlib

    import numpy as np

    out = dict(_drawn_inputs(seed))
    spreads = {}
    factors = {'attn_norm_g': 7.648, 'ssd_conv_b': 5.753, 'ssd_norm_g': 8.0, 'ffn_conv_b': 6.603}
    for name, (base, spread) in spreads.items():
        noise = np.random.default_rng([zlib.crc32(name.encode()), seed]).standard_normal(out[name].shape)
        drawn = base * np.exp(spread * noise) if base else spread * noise
        out[name] = __import__('jax').numpy.asarray(drawn.astype(out[name].dtype))
    for name, factor in factors.items():
        out[name] = (out[name] * factor).astype(out[name].dtype)
    return out
```

```python
from contextlib import ExitStack

import numpy as np

import concourse.bass as bass
from concourse import mybir

F32 = mybir.dt.float32
F32R = mybir.dt.float32r
I32 = mybir.dt.int32
ACT = mybir.ActivationFunctionType
ALU = mybir.AluOpType
AX_X = mybir.AxisListType.X

P = 128
D_MODEL, SEQ, DEPTH, PE_DIM = 2048, 256, 2, 256
HALVES = SEQ // P
KT = D_MODEL // P
CHUNK = 512
CHUNKS = D_MODEL // CHUNK
HEADS, HD = 8, 128
ATTN_WIDTH = HEADS * HD
SSD_HEADS, SSD_HD, SSD_GROUPS = 16, 64, 2
XBC_TILES, X_TILES, Z_TILES = 12, 8, 8
D_FF = 5632
FF_TILES = D_FF // P
FF1 = 24
FF2 = FF_TILES - FF1
ALPHA = float((2 * DEPTH) ** 0.25)
LN_EPS, RMS_EPS = 1e-5, 1e-6
SCALE = HD ** -0.5
UNIT = 2048

U_V = 0
U_XBC = U_V + 8
U_Z = U_XBC + XBC_TILES
U_QK = U_Z + Z_TILES
U_WS = U_QK + 16
U_WA = U_WS + 8
U_GP = U_WA + 8
U_UP1 = U_GP + 5 * CHUNKS
U_DN1 = U_UP1 + 2 * FF1
U_UP2 = U_DN1 + FF1 // 4 * CHUNKS
U_DN2 = U_UP2 + 2 * FF2
UNITS = U_DN2 + FF2 // 4 * CHUNKS
G_V = 0
G_XBC = G_V + 4
G_Z = G_XBC + XBC_TILES
G_QK = G_Z + Z_TILES
G_WS = G_QK + 8
G_WA = G_WS + 8
G_GP = G_WA + 8
G_UP1 = G_GP + 4 * CHUNKS
G_DN1 = G_UP1 + 2 * FF1
G_UP2 = G_DN1 + 2 * CHUNKS
G_DN2 = G_UP2 + 2 * FF2
GROUPS = G_DN2 + 2 * CHUNKS
RAW, RING, BANKS = 2, 4, 4
AHEAD = RING - 1
assert UNITS % RING == 0 and GROUPS % BANKS == 0

C_XW, C_XB, C_SN, C_AN, C_D = 0, 48, 60, 68, 76
C_L1G, C_L1B, C_L2G, C_L2B = 84, 100, 116, 132
C_FW, C_FB = 148, 148 + 3 * 2 * FF_TILES
COLS = C_FB + 2 * FF_TILES
K_ID, K_ONE, K_TRI, K_AMASK, K_SMASK, K_FREQ = 0, 128, 256, 384, 768, 1024
CONSTS = 1040
TWO_PI_PARTS = []
_rest = 2 * np.pi
for _bits in (2 ** -2, 2 ** -9, 2 ** -15, 2 ** -21):
    _part = float(np.floor(_rest / _bits) * _bits)
    TWO_PI_PARTS.append(_part)
    _rest -= _part
TWO_PI_PARTS.append(float(_rest))
ROUND = 1.5 * 2.0 ** 23
V_CHAIN = 1024
G_CHAIN = 256


def build(nc, x_tok, xT, pT, pos, weights, wdt, cols, rows, gb, consts, out):
    with ExitStack() as ctx:
        ctx.enter_context(nc.allow_non_contiguous_dma(reason="small parameter rows"))
        place = [(nc.sbuf_base + 31) // 32 * 32]

        def keep(name, shape, dt=F32):
            size = int(np.prod(shape[1:])) * 4
            t = nc.alloc_sbuf_tensor_at(name, shape, dt, offset=place[0])
            place[0] += (size + 31) // 32 * 32
            return t

        hT = keep("hT", [P, KT, 2 * SEQ], F32R)
        acc = keep("acc", [P, HALVES, D_MODEL])
        raw = [keep(f"raw{i}", [P, UNIT]) for i in range(RAW)]
        split = [keep(f"split{i}", [P, 2, UNIT], F32R) for i in range(RING)]
        cst = keep("cst", [P, CONSTS])
        col = keep("col", [P, COLS])
        row = keep("row", [P, 32])
        cos = keep("cos", [P, HALVES, 32])
        sin = keep("sin", [P, HALVES, 32])
        dtx = keep("dtx", [P, 12, 32])
        acs = keep("acs", [P, HALVES, 16])
        acsT = keep("acsT", [16, SEQ])
        stat = keep("stat", [P, 2, 8])
        bn = keep("bn", [P, HALVES, 6 * CHUNKS])
        ln = keep("ln", [P, HALVES, 6])
        xpad = [keep(f"xpad{i}", [P, 3 + SEQ]) for i in range(2)]
        region = place[0]

        def at(name, kib, shape, dt=F32):
            off = region + int(kib * 1024)
            assert off + int(np.prod(shape[1:])) * 4 <= nc.sbuf_usable_end, name
            return nc.alloc_sbuf_tensor_at(name, shape, dt, offset=off)

        xbT = at("xbT", 0, [P, X_TILES, SEQ])
        bcT = at("bcT", 8, [P, 4, SEQ])
        zs = at("zs", 12, [P, Z_TILES, SEQ])
        xdt = at("xdt", 20, [P, HALVES, 1024])
        cb = at("cb", 28, [P, SSD_GROUPS, 384])
        seg = [at(f"seg{i}", 31 + 1.5 * i, [P, 384]) for i in range(2)]
        mm = [at(f"mm{i}", 34 + 1.5 * i, [P, 384]) for i in range(2)]
        v_tok = at("v_tok", 37, [P, HALVES, ATTN_WIDTH])
        qk_tok = [at("qk_tok0", 8, [P, HALVES, CHUNK]), at("qk_tok1", 45, [P, HALVES, CHUNK])]
        qT = at("qT", 49, [P, HEADS, SEQ])
        kT = at("kT", 57, [P, HEADS, SEQ])
        sq = [at(f"sq{i}", 65 + i, [P, SEQ]) for i in range(2)]
        rms_s = at("rms_s", 67, [P, SEQ])
        rope = xpad[0][:, 3:3 + SEQ].rearrange("p (a n) -> p a n", a=2)
        tmp = xpad[1][:, 3:3 + SEQ]
        conv = [at(f"conv{i}", 49 + i, [P, SEQ]) for i in range(2)]
        oT = at("oT", 0, [P, HEADS, SEQ])
        sco = [at(f"sco{i}", 31 + 1.5 * i, [P, 384]) for i in range(2)]
        prT = [at(f"prT{i}", 34 + 1.5 * i, [P, 384]) for i in range(2)]
        wdt_raw = at("wdt_raw", 57, [P, KT, 16])
        wdt_s = at("wdt_s", 58, [P, KT, 32], F32R)
        lnf = [at(f"lnf{i}", 65 + i, [P, SEQ]) for i in range(2)]
        gbt = at("gbt", 61, [P, 2, CHUNK])
        sig = [at(f"sig{i}", 2 * i, [P, CHUNK]) for i in range(2)]
        gated = [at(f"gated{i}", 4 + 2 * i, [P, CHUNK]) for i in range(2)]
        p_raw = at("p_raw", 8, [P, 2, SEQ])
        p_s = at("p_s", 10, [P, 2, 2 * SEQ], F32R)
        ffT = at("ffT", 0, [P, FF1, 2 * SEQ], F32R)
        cv = [at(f"cv{i}", 48 + i, [P, SEQ]) for i in range(4)]
        gs = [at(f"gs{i}", 52 + i, [P, SEQ]) for i in range(2)]
        prod = [at(f"prod{i}", 54 + i, [P, SEQ]) for i in range(2)]
        x_st = at("x_st", 0, [P, KT, SEQ])
        ang = at("ang", 20, [P, 6, 32])
        posi = at("posi", 21, [P, HALVES], I32)

        gp = [ctx.enter_context(nc.psum_tensor(f"gp{i}", [P, 512], F32)) for i in range(BANKS)]
        xq = [ctx.enter_context(nc.psum_tensor(f"xq{i}", [P, 512], F32)) for i in range(4)]

        ident, ones, tri = cst[:, K_ID:K_ID + P], cst[:, K_ONE:K_ONE + P], cst[:, K_TRI:K_TRI + P]
        amask = cst[:, K_AMASK:K_AMASK + 384]
        smask = cst[:, K_SMASK:K_SMASK + 256]

        def sem(name):
            return ctx.enter_context(nc.semaphore(name))

        raw_in = [sem(f"raw_in{i}") for i in range(RAW)]
        start_in, x_in, par_in, p_in, gb_in, out_in = (sem(n) for n in (
            "start_in", "x_in", "par_in", "p_in", "gb_in", "out_in"))
        hi_done, lo_done, unit_used = sem("hi_done"), sem("lo_done"), sem("unit_used")
        gemm_evac = sem("gemm_evac")
        hT_ready, mixhi_done, mix_ready = sem("hT_ready"), sem("mixhi_done"), sem("mix_ready")
        v_chain, a_chain, g_chain = sem("v_chain"), sem("a_chain"), sem("g_chain")
        x_hi, ang_done, trig_done = sem("x_hi"), sem("ang_done"), sem("trig_done")
        wdt_hi, wdt_ready, dt_mm, dt_pre, dt_exp, a_exp = (sem(n) for n in (
            "wdt_hi", "wdt_ready", "dt_mm", "dt_pre", "dt_exp", "a_exp"))
        da_ready, acs_mm, acs_ready, acsT_mm, acsT_ready = (sem(n) for n in (
            "da_ready", "acs_mm", "acs_ready", "acsT_mm", "acsT_ready"))
        xconv_done, xsilu_done, zsilu_done, cb_mm, cb_ready, xt_mm, xdt_ready = (sem(n) for n in (
            "xconv_done", "xsilu_done", "zsilu_done", "cb_mm", "cb_ready", "xt_mm", "xdt_ready"))
        row_mm, seg_done, segexp_done, m_done, y_mm, y_read = (sem(n) for n in (
            "row_mm", "seg_done", "segexp_done", "m_done", "y_mm", "y_read"))
        yg_done, ysq_done, yrms_mm, yrms_read, yn_done = (sem(n) for n in (
            "yg_done", "ysq_done", "yrms_mm", "yrms_read", "yn_done"))
        orms_read, root_done = sem("orms_read"), sem("root_done")
        rope_done, qkT_mm, qkT_ready = sem("rope_done"), sem("qkT_mm"), sem("qkT_ready")
        sc_mm, sc_read, max_done, exp_done, prob_done = (sem(n) for n in (
            "sc_mm", "sc_read", "max_done", "exp_done", "prob_done"))
        prT_mm, prT_ready, o_mm, osq_done, orms_mm, on_done = (sem(n) for n in (
            "prT_mm", "prT_ready", "o_mm", "osq_done", "orms_mm", "on_done"))
        ln_norm, ln_mm, ln_aff, ln_res = (sem(n) for n in ("ln_norm", "ln_mm", "ln_aff", "ln_res"))
        p_hi, p_ready, sig_done = sem("p_hi"), sem("p_ready"), sem("sig_done")
        conv_done, silu_done, prod_done, ffhi_done, ff_ready = (sem(n) for n in (
            "conv_done", "silu_done", "prod_done", "ffhi_done", "ff_ready"))

        block = ctx.enter_context(nc.Block())

        @block.sync
        def _(sp):
            def load(n, slot):
                sp.dma_start(raw[slot][:, :], weights[n]).then_inc(raw_in[slot], 16)

            for n in range(RAW):
                load(n, n)
            with sp.Fori(1, DEPTH * UNITS // RAW) as u:
                for slot in range(RAW):
                    sp.wait_ge(lo_done, RAW * u + slot - RAW + 1)
                    sp.dma_start(raw[slot][:, :], weights[bass.ds(RAW * u + slot, 1)].rearrange("a p n -> p (a n)")
                                 ).then_inc(raw_in[slot], 16)
            sp.wait_ge(ln_res, 1 + DEPTH * 4 * CHUNKS)
            sp.dma_start(out, acc[:, :, :]).then_inc(out_in, 16)
            sp.wait_ge(out_in, 16)

        @block.gpsimd
        def _(pool):
            g = nc.gpsimd
            g.dma_start(cst[:, :], consts).then_inc(start_in, 16)
            g.dma_start(posi[:, :], pos).then_inc(start_in, 16)
            g.dma_start(x_st[:, :, :], xT).then_inc(x_in, 16)
            g.dma_start(acc[:, :, :], x_tok).then_inc(start_in, 16)

            pool.sem_inc(prod_done, 2)
            pool.sem_inc(ln_res, 1)
            pool.wait_ge(trig_done, 1)

            with pool.Fori(0, DEPTH) as l:
                count = [0]

                def link(ins):
                    count[0] += 1
                    ins.then_inc(g_chain, 1)
                    pool.wait_ge(g_chain, G_CHAIN * l + count[0])

                pool.wait_ge(hT_ready, 32 * l + 16)
                g.dma_start(col[:, :], cols[bass.ds(l, 1)].rearrange("a p n -> p (a n)")).then_inc(par_in, 16)
                g.dma_start(row[:, :], rows[bass.ds(l, 1)].rearrange("a p n -> p (a n)")).then_inc(par_in, 16)
                g.dma_start(wdt_raw[:, :, :], wdt[bass.ds(l, 1)].rearrange("a p k n -> p (a k) n")).then_inc(par_in, 16)

                def ssd_product(h):
                    pool.wait_ge(segexp_done, SSD_HEADS * l + h + 1)
                    if h == 0:
                        pool.wait_ge(cb_ready, SSD_GROUPS * l + 2)
                    if h >= 2:
                        pool.wait_ge(y_mm, SSD_HEADS * l + h - 1)
                    g.tensor_tensor(mm[h % 2][:, :], seg[h % 2][:, :], cb[:, h // 8, :], ALU.mult).then_inc(m_done, 1)

                def rotate(c):
                    for half in range(HALVES):
                        pool.wait_ge(gemm_evac, BANKS + GROUPS * l + G_QK + 2 * c + half + 1)
                        if c or half:
                            pool.wait_ge(rope_done, 8 * l + 2 * c + half)
                        t = qk_tok[c % 2][:, half, :].rearrange("p (h d) -> p h d", d=HD)
                        cs = cos[:, half, :].unsqueeze(1).to_broadcast([P, 4, 32])
                        sn = sin[:, half, :].unsqueeze(1).to_broadcast([P, 4, 32])
                        a = rope[:, 0, :].rearrange("p (h d) -> p h d", d=32)
                        b = rope[:, 1, :].rearrange("p (h d) -> p h d", d=32)
                        g.tensor_tensor(a, t[:, :, 0:32], cs, ALU.mult)
                        g.tensor_tensor(b[:, :, 0:16], t[:, :, 16:32], sn[:, :, 0:16], ALU.mult)
                        link(g.tensor_tensor(b[:, :, 16:32], t[:, :, 0:16], sn[:, :, 16:32], ALU.mult))
                        g.tensor_tensor(t[:, :, 0:32], a, b, ALU.add).then_inc(rope_done, 1)

                for h in range(SSD_HEADS):
                    ssd_product(h)
                    if h % 4 == 3:
                        rotate(h // 4)

                pool.wait_ge(mix_ready, 4 * l + 4)
                g.dma_start(p_raw[:, :, :], pT[bass.ds(l, 1)].rearrange("a p k n -> p (a k) n")).then_inc(p_in, 16)

                def residual(which):
                    for c in range(CHUNKS):
                        if c:
                            pool.wait_ge(ln_res, 1 + (2 * l + which) * 2 * CHUNKS + 2 * c)
                        g.dma_start(gbt[:, :, :], gb[bass.ds(2 * l + which, 1), :, c * CHUNK:(c + 1) * CHUNK]
                                    .to_broadcast([P, 2, CHUNK])).then_inc(gb_in, 16)
                        if c == 0:
                            pool.wait_ge(ln_mm, 32 * l + 16 * which + 16)
                        pool.wait_ge(gb_in, 16 * ((2 * l + which) * CHUNKS + c + 1))
                        for half in range(HALVES):
                            t = acc[:, half, c * CHUNK:(c + 1) * CHUNK]
                            link(g.tensor_tensor(t, t, gbt[:, 0, :], ALU.mult))
                            g.tensor_tensor(t, t, gbt[:, 1, :], ALU.add).then_inc(ln_res, 1)

                residual(0)

                def ff_pair(pair, b, again=True):
                    pool.wait_ge(silu_done, FF_TILES * l + pair + 1)
                    pool.wait_ge(conv_done, 2 * FF_TILES * l + 2 * pair + 2)
                    if again:
                        pool.wait_ge(ff_ready, FF_TILES * l + pair - 1)
                    g.tensor_tensor(prod[b][:, :], gs[b][:, :], cv[2 * b + 1][:, :], ALU.mult).then_inc(prod_done, 1)

                def ff_lo(pair, b, kt):
                    pool.wait_ge(ffhi_done, FF_TILES * l + pair + 1)
                    g.tensor_tensor(ffT[:, kt, SEQ:2 * SEQ], prod[b][:, :],
                                    ffT[:, kt, 0:SEQ].bitcast(F32), ALU.subtract).then_inc(ff_ready, 1)

                for first, tiles in ((0, FF1), (FF1, FF2)):
                    ff_pair(first, 0, first > 0)
                    ff_pair(first + 1, 1, first > 0)
                    with pool.Fori(0, tiles // 2 - 1) as u:
                        for b in range(2):
                            pool.wait_ge(ffhi_done, FF_TILES * l + first + 2 * u + b + 1)
                            g.tensor_tensor(ffT[:, bass.ds(2 * u + b, 1), SEQ:2 * SEQ].rearrange("p a n -> p (a n)"),
                                            prod[b][:, :],
                                            ffT[:, bass.ds(2 * u + b, 1), 0:SEQ].rearrange("p a n -> p (a n)")
                                            .bitcast(F32), ALU.subtract).then_inc(ff_ready, 1)
                            ff_pair(first + 2 * u + 2 + b, b)
                    ff_lo(first + tiles - 2, 0, tiles - 2)
                    ff_lo(first + tiles - 1, 1, tiles - 1)
                residual(1)
                pool.sem_inc(g_chain, G_CHAIN - count[0])

        @block.scalar
        def _(act):
            s = nc.scalar

            act.wait_ge(x_in, 16)
            s.activation(hT[:, :, 0:SEQ], x_st[:, :, :], ACT.Copy).then_inc(x_hi, 1)
            act.wait_ge(ang_done, 1)
            s.activation(sin[:, :, 0:16], ang[:, 0, :].rearrange("p (h f) -> p h f", f=16), ACT.Sin, scale=-1.0)
            s.activation(sin[:, :, 16:32], ang[:, 0, :].rearrange("p (h f) -> p h f", f=16), ACT.Sin)
            s.activation(cos[:, :, 0:16], ang[:, 1, :].rearrange("p (h f) -> p h f", f=16), ACT.Sin)
            s.activation(cos[:, :, 16:32], ang[:, 1, :].rearrange("p (h f) -> p h f", f=16), ACT.Sin
                         ).then_inc(trig_done, 1)

            with act.Fori(0, DEPTH) as l:

                def hi(i, u=None, step=0):
                    more, more_raw = (0, 0) if u is None else (step * u, step // RAW * u)
                    act.wait_ge(raw_in[i % RAW], 16 * (UNITS // RAW * l + more_raw + i // RAW + 1))
                    act.wait_ge(unit_used, UNITS * l + more + i + 1)
                    s.activation(split[i % RING][:, 0, :], raw[i % RAW][:, :], ACT.Copy).then_inc(hi_done, 1)

                for i in range(AHEAD):
                    hi(i)
                for i in range(U_V, U_XBC):
                    if i == U_V + 5:
                        act.wait_ge(par_in, 48 * l + 48)
                        s.activation(wdt_s[:, :, 0:16], wdt_raw[:, :, :], ACT.Copy).then_inc(wdt_hi, 1)
                    hi(i + AHEAD)
                s.activation(row[:, 16:32], row[:, 16:32], ACT.Exp).then_inc(a_exp, 1)
                act.wait_ge(dt_pre, l + 1)
                s.activation(dtx[:, 2, :], dtx[:, 1, :], ACT.Exp, scale=-1.0).then_inc(dt_exp, 1)

                for j in range(XBC_TILES):
                    hi(U_XBC + j + AHEAD)
                    act.wait_ge(xconv_done, XBC_TILES * l + j + 1)
                    dst = bcT[:, j, :] if j < 4 else xbT[:, j - 4, :]
                    s.activation(dst, conv[j % 2][:, :], ACT.Silu).then_inc(xsilu_done, 1)
                for j in range(Z_TILES):
                    hi(U_Z + j + AHEAD)
                    act.wait_ge(gemm_evac, BANKS + GROUPS * l + G_Z + j + 1)
                    s.activation(zs[:, j, :], zs[:, j, :], ACT.Silu).then_inc(zsilu_done, 1)

                def y_square(j):
                    act.wait_ge(yg_done, X_TILES * l + j + 1)
                    if j >= 2:
                        act.wait_ge(yrms_mm, X_TILES * l + j - 1)
                    s.activation(sq[j % 2][:, :], zs[:, j, :], ACT.Square).then_inc(ysq_done, 1)

                def inverse_root(n):
                    s.activation(tmp, rms_s[:, :], ACT.Ln).then_inc(a_chain, 1)
                    act.wait_ge(a_chain, 3 * l + n + 1)
                    s.activation(tmp, tmp, ACT.Exp, scale=-0.5).then_inc(root_done, 1)

                def qkT_evac(c, b):
                    act.wait_ge(qkT_mm, 8 * l + 2 * c + b + 1)
                    dst, h0 = (kT if c % 2 else qT), 4 * (c // 2) + 2 * b
                    s.activation(dst[:, h0:h0 + 2, :], xq[3][:, :].rearrange("p (h t) -> p h t", h=2), ACT.Copy
                                 ).then_inc(qkT_ready, 1)

                for h in range(SSD_HEADS):
                    act.wait_ge(seg_done, SSD_HEADS * l + h + 1)
                    s.activation(seg[h % 2][:, :], seg[h % 2][:, :], ACT.Exp).then_inc(segexp_done, 1)
                    if h >= 3 and h % 2:
                        y_square(h // 2 - 1)
                    if h == 11:
                        act.wait_ge(yrms_read, SSD_GROUPS * l + 1)
                        inverse_root(0)
                    if h == 10:
                        act.wait_ge(ln_res, 1 + 4 * CHUNKS * l)
                    if h >= 6 and h % 4 >= 2:
                        qkT_evac((h - 6) // 4, h % 4 - 2)
                    hi(U_QK + h + AHEAD)

                def mix_hi(n, src):
                    s.activation(hT[:, 4 * n:4 * n + 4, 0:SEQ], src, ACT.Copy).then_inc(mixhi_done, 1)

                act.wait_ge(yn_done, X_TILES * l + 4)
                act.wait_ge(unit_used, RING + UNITS * l + U_WS)
                mix_hi(2, zs[:, 0:4, :])
                y_square(X_TILES - 1)
                act.wait_ge(yrms_read, SSD_GROUPS * l + 2)
                inverse_root(1)

                def head_exp(h):
                    act.wait_ge(max_done, HEADS * l + h + 1)
                    t, st = sco[h % 2], stat[:, h % 2, :]
                    s.activation(t[:, 0:128], t[:, 0:128], ACT.Exp, bias=st[:, 0:1], accum_out=st[:, 2:3])
                    s.activation(t[:, 128:384], t[:, 128:384], ACT.Exp, bias=st[:, 1:2], accum_out=st[:, 3:4]
                                 ).then_inc(exp_done, 1)

                def head_prT(h):
                    act.wait_ge(prT_mm, HEADS * l + h + 1)
                    if h >= 2:
                        act.wait_ge(o_mm, HEADS * l + h - 1)
                    s.activation(prT[h % 2][:, :], xq[1][:, 0:384], ACT.Copy).then_inc(prT_ready, 1)

                def head_out(h):
                    act.wait_ge(o_mm, HEADS * l + h + 1)
                    if h >= 2:
                        act.wait_ge(orms_mm, HEADS * l + h - 1)
                    s.activation(oT[:, h, :], xq[2][:, 0:SEQ], ACT.Copy)
                    s.activation(sq[h % 2][:, :], xq[2][:, 0:SEQ], ACT.Square).then_inc(osq_done, 1)

                qkT_evac(3, 0)
                for h in range(HEADS):
                    if h == 0:
                        act.wait_ge(yn_done, X_TILES * l + 8)
                        mix_hi(3, zs[:, 4:8, :])
                    head_exp(h)
                    if h == 0:
                        qkT_evac(3, 1)
                    if h >= 2:
                        head_out(h - 2)
                    if h >= 1:
                        head_prT(h - 1)
                    hi(U_WS + h + AHEAD)
                head_out(HEADS - 2)
                head_prT(HEADS - 1)
                head_out(HEADS - 1)
                act.wait_ge(orms_read, l + 1)
                inverse_root(2)
                for n in range(2):
                    act.wait_ge(on_done, HEADS * l + 4 * n + 4)
                    if n == 0:
                        act.wait_ge(unit_used, RING + UNITS * l + U_WS)
                    mix_hi(n, oT[:, 4 * n:4 * n + 4, :])
                for i in range(U_WA, U_GP):
                    hi(i + AHEAD)

                def affine(which):
                    for kt in range(KT):
                        act.wait_ge(ln_mm, 2 * KT * l + KT * which + kt + 1)
                        if kt >= 2:
                            act.wait_ge(hT_ready, KT + 2 * KT * l + KT * which + kt - 1)
                        gc = (C_L1G if which == 0 else C_L2G) + kt
                        s.activation(lnf[kt % 2][:, :], xq[kt % 4][:, 0:SEQ], ACT.Identity,
                                     scale=col[:, gc:gc + 1], bias=col[:, gc + KT:gc + KT + 1]).then_inc(ln_aff, 1)

                affine(0)
                for c in range(CHUNKS):
                    for r in range(5):
                        if c == 0 and r == 2:
                            act.wait_ge(p_in, 16 * l + 16)
                            s.activation(p_s[:, :, 0:SEQ], p_raw[:, :, :], ACT.Copy).then_inc(p_hi, 1)
                        if r == 4:
                            for half in range(HALVES):
                                act.wait_ge(unit_used, RING + UNITS * l + U_GP + 5 * c + 4)
                                if c:
                                    act.wait_ge(gemm_evac, BANKS + GROUPS * l + G_GP + 4 * c)
                                s.activation(sig[half][:, :], gp[half][:, :], ACT.Sigmoid).then_inc(sig_done, 1)
                        hi(U_GP + 5 * c + r + AHEAD)

                def silu(pair, b):
                    act.wait_ge(conv_done, 2 * FF_TILES * l + 2 * pair + 1)
                    act.wait_ge(prod_done, FF_TILES * l + pair + 1)
                    s.activation(gs[b][:, :], cv[2 * b][:, :], ACT.Silu).then_inc(silu_done, 1)

                for first, tiles, u0, d0 in ((0, FF1, U_UP1, U_DN1), (FF1, FF2, U_UP2, U_DN2)):
                    hi(u0 + AHEAD)
                    silu(first, 0)
                    hi(u0 + 1 + AHEAD)
                    with act.Fori(0, tiles // 2 - 1) as u:
                        for b in range(2):
                            i = u0 + 2 + 2 * b
                            act.wait_ge(prod_done, FF_TILES * l + 2 * u + (first + b + 3))
                            s.activation(ffT[:, bass.ds(2 * u + b, 1), 0:SEQ].rearrange("p a n -> p (a n)"),
                                         prod[b][:, :], ACT.Copy).then_inc(ffhi_done, 1)
                            hi(i + AHEAD, u, 4)
                            silu(2 * u + (first + b + 1), (b + 1) % 2)
                            hi(i + 1 + AHEAD, u, 4)
                    last = tiles - 2
                    act.wait_ge(prod_done, FF_TILES * l + first + last + 3)
                    s.activation(ffT[:, last, 0:SEQ], prod[0][:, :], ACT.Copy).then_inc(ffhi_done, 1)
                    hi(u0 + 2 * last + 2 + AHEAD)
                    silu(first + last + 1, 1)
                    hi(u0 + 2 * last + 3 + AHEAD)
                    act.wait_ge(prod_done, FF_TILES * l + first + last + 4)
                    s.activation(ffT[:, last + 1, 0:SEQ], prod[1][:, :], ACT.Copy).then_inc(ffhi_done, 1)
                    if first == 0:
                        with act.Fori(0, 2) as u:
                            for r in range(12):
                                hi(d0 + r + AHEAD, u, 12)
                        act.wait_ge(unit_used, RING + UNITS * l + U_UP2)
                    else:
                        for i in range(d0, UNITS - AHEAD):
                            hi(i + AHEAD)
                affine(1)

        @block.vector
        def _(dve):
            v = nc.vector

            dve.sem_inc(gemm_evac, BANKS)
            for t in xpad:
                v.memset(t[:, 0:3], 0.0)
            dve.wait_ge(x_hi, 1)
            for kt in range(KT):
                v.tensor_tensor(hT[:, kt, SEQ:2 * SEQ], x_st[:, kt, :], hT[:, kt, 0:SEQ].bitcast(F32), ALU.subtract
                                ).then_inc(hT_ready, 1)

            start = [0]

            def first(ins):
                start[0] += 1
                ins.then_inc(v_chain, 1)
                dve.wait_ge(v_chain, start[0])

            dve.wait_ge(start_in, 48)
            first(v.tensor_copy(ang[:, 5, 0:2], posi[:, :]))
            for half in range(HALVES):
                last = v.tensor_scalar(ang[:, 2, half * 16:half * 16 + 16], cst[:, K_FREQ:K_FREQ + 16],
                                       ang[:, 5, half:half + 1], None, ALU.mult)
            first(last)
            first(v.tensor_scalar(ang[:, 3, :], ang[:, 2, :], float(1 / (2 * np.pi)), None, ALU.mult))
            first(v.tensor_scalar(ang[:, 3, :], ang[:, 3, :], ROUND, None, ALU.add))
            first(v.tensor_scalar(ang[:, 3, :], ang[:, 3, :], ROUND, None, ALU.subtract))
            for part in TWO_PI_PARTS:
                first(v.scalar_tensor_tensor(ang[:, 2, :], ang[:, 3, :], -part, ang[:, 2, :], ALU.mult, ALU.add))
            PI = 3.1415925
            first(v.tensor_scalar(ang[:, 0, :], ang[:, 2, :], PI, -PI, ALU.min, ALU.max))
            first(v.tensor_scalar(ang[:, 2, :], ang[:, 2, :], float(np.pi / 2), None, ALU.add))
            first(v.tensor_scalar(ang[:, 4, :], ang[:, 2, :], float(np.pi), -float(2 * np.pi), ALU.is_gt, ALU.mult))
            first(v.tensor_tensor(ang[:, 2, :], ang[:, 2, :], ang[:, 4, :], ALU.add))
            v.tensor_scalar(ang[:, 1, :], ang[:, 2, :], PI, -PI, ALU.min, ALU.max).then_inc(ang_done, 1)

            with dve.Fori(0, DEPTH) as l:
                count = [start[0]]

                def link(ins):
                    count[0] += 1
                    ins.then_inc(v_chain, 1)
                    dve.wait_ge(v_chain, V_CHAIN * l + count[0])

                def lo(i, u=None, step=0):
                    more = 0 if u is None else step * u
                    dve.wait_ge(hi_done, UNITS * l + more + i + 1)
                    v.tensor_tensor(split[i % RING][:, 1, :], raw[i % RAW][:, :],
                                    split[i % RING][:, 0, :].bitcast(F32), ALU.subtract).then_inc(lo_done, 1)

                def group(g, i, more=0):
                    dve.wait_ge(unit_used, UNITS * l + more + (RING + i + 1))
                    return gp[g % BANKS]

                def sum_parts(g, i, dst, more=0):
                    bank = group(g, i, more)
                    v.tensor_reduce(dst, bank[:, :].rearrange("p (a t) -> p t a", a=2), AX_X, ALU.add
                                    ).then_inc(gemm_evac, 1)

                for i in range(AHEAD):
                    lo(i)
                for c in range(2):
                    for r in range(4):
                        if r == 0 and c:
                            for half in range(HALVES):
                                v.tensor_copy(v_tok[:, half, 0:CHUNK], group(half, U_V + 3)[:, :]).then_inc(gemm_evac, 1)
                        if c == 1 and r == 2:
                            dve.wait_ge(wdt_hi, l + 1)
                            v.tensor_tensor(wdt_s[:, :, 16:32], wdt_raw[:, :, :], wdt_s[:, :, 0:16].bitcast(F32),
                                            ALU.subtract).then_inc(wdt_ready, 1)
                        lo(U_V + 4 * c + r + AHEAD)
                for half in range(HALVES):
                    v.tensor_copy(v_tok[:, half, CHUNK:2 * CHUNK], group(2 + half, U_V + 7)[:, :]).then_inc(gemm_evac, 1)

                dve.wait_ge(dt_mm, l + 1)
                link(v.tensor_reduce(dtx[:, 0, :].rearrange("p (h n) -> p h n", n=16),
                                     xq[0][:, 0:64].rearrange("p (h a n) -> p h n a", h=2, a=2), AX_X, ALU.add))
                for half in range(HALVES):
                    t = dtx[:, 0, 16 * half:16 * half + 16]
                    last = v.tensor_tensor(t, t, row[:, 0:16], ALU.add)
                link(last)
                v.scalar_tensor_tensor(dtx[:, 1, :], dtx[:, 0, :], -1.0, dtx[:, 0, :], ALU.mult, ALU.max).then_inc(dt_pre, 1)
                dve.wait_ge(dt_exp, l + 1)
                link(v.tensor_scalar(dtx[:, 3, :], dtx[:, 2, :], 2.0, None, ALU.add))
                link(v.reciprocal(dtx[:, 4, :], dtx[:, 3, :]))
                link(v.tensor_tensor(dtx[:, 5, :], dtx[:, 4, :], dtx[:, 2, :], ALU.mult))
                link(v.tensor_tensor(dtx[:, 6, :], dtx[:, 5, :], dtx[:, 5, :], ALU.mult))
                link(v.tensor_scalar(dtx[:, 7, :], dtx[:, 6, :], 1.0 / 17, None, ALU.mult))
                for n in (15, 13, 11, 9, 7, 5, 3):
                    link(v.scalar_tensor_tensor(dtx[:, 7, :], dtx[:, 7, :], 1.0 / n, dtx[:, 6, :], ALU.add, ALU.mult))
                v.scalar_tensor_tensor(dtx[:, 8, :], dtx[:, 7, :], 1.0, dtx[:, 5, :], ALU.add, ALU.mult)
                link(v.tensor_scalar(dtx[:, 9, :], dtx[:, 0, :], 0.0, None, ALU.max))
                link(v.scalar_tensor_tensor(dtx[:, 10, :], dtx[:, 8, :], 2.0, dtx[:, 9, :], ALU.mult, ALU.add))
                dve.wait_ge(a_exp, l + 1)
                for half in range(HALVES):
                    v.scalar_tensor_tensor(dtx[:, 11, 16 * half:16 * half + 16], dtx[:, 10, 16 * half:16 * half + 16],
                                           -1.0, row[:, 16:32], ALU.mult, ALU.mult).then_inc(da_ready, 1)

                def taps(xp, o, w, n, b):
                    link(v.tensor_scalar(o[:, :], xp[:, 3:3 + SEQ], w(n - 1), b, ALU.mult, ALU.add))
                    for k in range(n - 1):
                        last = v.scalar_tensor_tensor(o[:, :], xp[:, 4 - n + k:4 - n + k + SEQ], w(k), o[:, :],
                                                      ALU.mult, ALU.add)
                        if k < n - 2:
                            link(last)
                    return last

                for j in range(XBC_TILES):
                    xp, o = xpad[j % 2], conv[j % 2]
                    sum_parts(G_XBC + j, U_XBC + j, xp[:, 3:3 + SEQ])
                    dve.wait_ge(gemm_evac, BANKS + GROUPS * l + G_XBC + j + 1)
                    if j >= 2:
                        dve.wait_ge(xsilu_done, XBC_TILES * l + j - 1)
                    taps(xp, o, lambda k: col[:, C_XW + 4 * j + k:C_XW + 4 * j + k + 1], 4,
                         col[:, C_XB + j:C_XB + j + 1]).then_inc(xconv_done, 1)
                    if j == 3:
                        dve.wait_ge(acs_mm, l + 1)
                        v.tensor_copy(acs[:, :, :], xq[1][:, 0:32].rearrange("p (h n) -> p h n", h=2)
                                      ).then_inc(acs_ready, 1)
                    if j == 6:
                        dve.wait_ge(acsT_mm, l + 1)
                        v.tensor_copy(acsT[:, :], xq[2][0:16, 0:SEQ]).then_inc(acsT_ready, 1)
                    lo(U_XBC + j + AHEAD)

                for j in range(Z_TILES):
                    sum_parts(G_Z + j, U_Z + j, zs[:, j, :])
                    if j in (1, 2):
                        dve.wait_ge(cb_mm, SSD_GROUPS * l + j)
                        v.tensor_copy(cb[:, j - 1, :], xq[j][:, 0:384]).then_inc(cb_ready, 1)
                    if 3 <= j < 7:
                        half, q = (j - 3) // 2, (j - 3) % 2
                        dve.wait_ge(xt_mm, 4 * l + j - 2)
                        v.tensor_tensor(xdt[:, half, CHUNK * q:CHUNK * (q + 1)].rearrange("p (h d) -> p h d", d=SSD_HD),
                                        xq[3][:, :].rearrange("p (h d) -> p h d", d=SSD_HD),
                                        dtx[:, 10, 16 * half + 8 * q:16 * half + 8 * q + 8].unsqueeze(2)
                                        .to_broadcast([P, 8, SSD_HD]), ALU.mult).then_inc(xdt_ready, 1)
                    lo(U_Z + j + AHEAD)

                def qk_out(c):
                    for half in range(HALVES):
                        if c >= 2:
                            dve.wait_ge(qkT_mm, 8 * l + 2 * c - 2)
                        v.tensor_copy(qk_tok[c % 2][:, half, :], group(G_QK + 2 * c + half, U_QK + 4 * c + 3)[:, :]
                                      ).then_inc(gemm_evac, 1)

                def y_gate(j):
                    dve.wait_ge(y_mm, SSD_HEADS * l + 2 * j + 2)
                    v.scalar_tensor_tensor(tmp, xbT[:, j, :], col[:, C_D + j:C_D + j + 1], xq[1][:, 0:SEQ],
                                           ALU.mult, ALU.add).then_inc(y_read, 1)
                    dve.wait_ge(y_read, X_TILES * l + j + 1)
                    dve.wait_ge(zsilu_done, Z_TILES * l + j + 1)
                    v.tensor_tensor(zs[:, j, :], zs[:, j, :], tmp, ALU.mult).then_inc(yg_done, 1)

                def inverse_root(n):
                    dve.wait_ge(root_done, 3 * l + n + 1)
                    link(v.scalar_tensor_tensor(rms_s[:, :], rms_s[:, :], -0.5, tmp, ALU.mult, ALU.mult))
                    link(v.tensor_tensor(rms_s[:, :], rms_s[:, :], tmp, ALU.mult))
                    link(v.scalar_tensor_tensor(rms_s[:, :], rms_s[:, :], 1.5, tmp, ALU.add, ALU.mult))

                def y_norm(g):
                    dve.wait_ge(yrms_mm, X_TILES * l + 4 * g + 4)
                    v.tensor_scalar(rms_s[:, :], xq[2][:, 0:SEQ], 1.0 / 512, RMS_EPS, ALU.mult, ALU.add
                                    ).then_inc(yrms_read, 1)
                    inverse_root(g)
                    for j in range(4 * g, 4 * g + 4):
                        v.scalar_tensor_tensor(zs[:, j, :], zs[:, j, :], col[:, C_SN + j:C_SN + j + 1], rms_s[:, :],
                                               ALU.mult, ALU.mult).then_inc(yn_done, 1)

                for h in range(SSD_HEADS):
                    if h and h % 4 == 0:
                        qk_out(h // 4 - 1)
                    dve.wait_ge(row_mm, SSD_HEADS * l + h + 1)
                    if h >= 2:
                        dve.wait_ge(m_done, SSD_HEADS * l + h - 1)
                    v.scalar_tensor_tensor(seg[h % 2][:, 0:256], xq[0][:, 0:256], acs[:, 0, h:h + 1], smask[:, 0:256],
                                           ALU.subtract, ALU.add)
                    v.scalar_tensor_tensor(seg[h % 2][:, 256:384], xq[0][:, 128:256], acs[:, 1, h:h + 1],
                                           smask[:, 0:128], ALU.subtract, ALU.add).then_inc(seg_done, 1)
                    if h >= 3 and h % 2:
                        y_gate(h // 2 - 1)
                    if h == 11:
                        y_norm(0)
                    lo(U_QK + h + AHEAD)
                qk_out(3)

                def mix_lo(n, src, m):
                    dve.wait_ge(mixhi_done, 4 * l + m + 1)
                    v.tensor_tensor(hT[:, 4 * n:4 * n + 4, SEQ:2 * SEQ], src, hT[:, 4 * n:4 * n + 4, 0:SEQ]
                                    .bitcast(F32), ALU.subtract).then_inc(mix_ready, 1)

                y_gate(X_TILES - 1)
                mix_lo(2, zs[:, 0:4, :], 0)
                y_norm(1)

                def head_scores(h):
                    t, st = sco[h % 2], stat[:, h % 2, :]
                    dve.wait_ge(sc_mm, HEADS * l + h + 1)
                    if h == 0:
                        dve.wait_ge(m_done, SSD_HEADS * l + SSD_HEADS)
                    if h >= 2:
                        dve.wait_ge(prT_mm, HEADS * l + h - 1)
                    v.scalar_tensor_tensor(t[:, :], xq[0][:, 0:384], SCALE, amask, ALU.mult, ALU.add
                                           ).then_inc(sc_read, 1)
                    dve.wait_ge(sc_read, HEADS * l + h + 1)
                    v.tensor_reduce(st[:, 0:1], t[:, 0:128], AX_X, ALU.max, negate=True)
                    v.tensor_reduce(st[:, 1:2], t[:, 128:384], AX_X, ALU.max, negate=True).then_inc(max_done, 1)

                def head_probs(h):
                    t, st = sco[h % 2], stat[:, h % 2, :]
                    dve.wait_ge(exp_done, HEADS * l + h + 1)
                    link(v.reciprocal(st[:, 4:6], st[:, 2:4]))
                    v.tensor_scalar(t[:, 0:128], t[:, 0:128], st[:, 4:5], None, ALU.mult)
                    v.tensor_scalar(t[:, 128:384], t[:, 128:384], st[:, 5:6], None, ALU.mult).then_inc(prob_done, 1)

                def out_rows(g, i, c, half, keep_scale, more=0, dc=None):
                    bank = group(g, i, more)
                    t = (acc[:, half, c * CHUNK:(c + 1) * CHUNK] if dc is None
                         else acc[:, half, bass.ds(dc + c * CHUNK, CHUNK)])
                    if keep_scale:
                        v.scalar_tensor_tensor(t, t, ALPHA, bank[:, :], ALU.mult, ALU.add).then_inc(gemm_evac, 1)
                    else:
                        v.tensor_tensor(t, t, bank[:, :], ALU.add).then_inc(gemm_evac, 1)

                for h in range(HEADS):
                    if h and h % 2 == 0:
                        for half in range(HALVES):
                            if h == 2:
                                dve.wait_ge(ln_res, 1 + 4 * CHUNKS * l)
                            out_rows(G_WS + h - 2 + half, U_WS + h - 1, h // 2 - 1, half, True)
                    head_scores(h)
                    if h == 0:
                        mix_lo(3, zs[:, 4:8, :], 1)
                    lo(U_WS + h + AHEAD)
                    head_probs(h)
                for half in range(HALVES):
                    out_rows(G_WS + 6 + half, U_WS + 7, 3, half, True)

                dve.wait_ge(orms_mm, HEADS * l + HEADS)
                v.tensor_scalar(rms_s[:, :], xq[3][:, 0:SEQ], 1.0 / ATTN_WIDTH, RMS_EPS, ALU.mult, ALU.add
                                ).then_inc(orms_read, 1)
                inverse_root(2)
                for h in range(HEADS):
                    v.scalar_tensor_tensor(oT[:, h, :], oT[:, h, :], col[:, C_AN + h:C_AN + h + 1], rms_s[:, :],
                                           ALU.mult, ALU.mult).then_inc(on_done, 1)
                for n in range(2):
                    mix_lo(n, oT[:, 4 * n:4 * n + 4, :], 2 + n)

                def rows_and_stats(g, i, c):
                    for half in range(HALVES):
                        out_rows(g + half, i, c, half, False)
                    for half in range(HALVES):
                        dve.wait_ge(gemm_evac, BANKS + GROUPS * l + g + half + 1)
                        last = v.bn_stats(bn[:, half, 6 * c:6 * c + 6], acc[:, half, c * CHUNK:(c + 1) * CHUNK])
                    return last

                def layer_norm(which):
                    v.memset(ln[:, :, 5], 0.0)
                    for half in range(HALVES):
                        last = v.bn_aggr(ln[:, half, 0:2], bn[:, half, :])
                    link(last)
                    link(v.tensor_scalar(ln[:, :, 4], ln[:, :, 1], LN_EPS, None, ALU.add))
                    link(v.tensor_scalar(ln[:, :, 5].bitcast(I32), ln[:, :, 4].bitcast(I32), 1, None,
                                         ALU.arith_shift_right))
                    link(v.tensor_scalar(ln[:, :, 2].bitcast(I32), ln[:, :, 5].bitcast(I32), -1.0, float(0x5f3759df),
                                         ALU.mult, ALU.add))
                    for _ in range(4):
                        link(v.scalar_tensor_tensor(ln[:, :, 5], ln[:, :, 2], -0.5, ln[:, :, 4], ALU.mult, ALU.mult))
                        link(v.tensor_tensor(ln[:, :, 5], ln[:, :, 5], ln[:, :, 2], ALU.mult))
                        link(v.scalar_tensor_tensor(ln[:, :, 2], ln[:, :, 5], 1.5, ln[:, :, 2], ALU.add, ALU.mult))
                    link(v.scalar_tensor_tensor(ln[:, :, 3], ln[:, :, 0], -1.0, ln[:, :, 2], ALU.mult, ALU.mult))
                    for c in range(CHUNKS):
                        for half in range(HALVES):
                            t = acc[:, half, c * CHUNK:(c + 1) * CHUNK]
                            last = v.tensor_scalar(t, t, ln[:, half, 2:3], ln[:, half, 3:4], ALU.mult, ALU.add)
                        last.then_inc(ln_norm, 1)
                    for kt in range(KT):
                        dve.wait_ge(ln_aff, 2 * KT * l + KT * which + kt + 1)
                        link(v.tensor_copy(hT[:, kt, 0:SEQ], lnf[kt % 2][:, :]))
                        v.tensor_tensor(hT[:, kt, SEQ:2 * SEQ], lnf[kt % 2][:, :], hT[:, kt, 0:SEQ].bitcast(F32),
                                        ALU.subtract).then_inc(hT_ready, 1)

                for c in range(CHUNKS):
                    lo(U_WA + 2 * c + AHEAD)
                    if c:
                        rows_and_stats(G_WA + 2 * c - 2, U_WA + 2 * c - 1, c - 1)
                    lo(U_WA + 2 * c + 1 + AHEAD)
                link(rows_and_stats(G_WA + 6, U_WA + 7, 3))
                layer_norm(0)

                def gate_rows(c):
                    dve.wait_ge(sig_done, 2 * CHUNKS * l + 2 * c + 2)
                    for half in range(HALVES):
                        bank = group(G_GP + 4 * c + 2 + half, U_GP + 5 * c + 4)
                        v.tensor_tensor(gated[half][:, :], bank[:, :], sig[half][:, :], ALU.mult).then_inc(gemm_evac, 2)
                        dve.wait_ge(gemm_evac, BANKS + GROUPS * l + G_GP + 4 * c + 2 * half + 2)
                        dve.wait_ge(ln_res, 1 + 4 * CHUNKS * l + 2 * c + half + 1)
                        t = acc[:, half, c * CHUNK:(c + 1) * CHUNK]
                        last = v.scalar_tensor_tensor(t, t, ALPHA, gated[half][:, :], ALU.mult, ALU.add)
                    if c < CHUNKS - 1:
                        link(last)

                for c in range(CHUNKS):
                    for r in range(5):
                        if c == 0 and r == 3:
                            dve.wait_ge(p_hi, l + 1)
                            v.tensor_tensor(p_s[:, :, SEQ:2 * SEQ], p_raw[:, :, :], p_s[:, :, 0:SEQ].bitcast(F32),
                                            ALU.subtract).then_inc(p_ready, 1)
                        if c and r == 1:
                            gate_rows(c - 1)
                        lo(U_GP + 5 * c + r + AHEAD)
                gate_rows(CHUNKS - 1)

                for first_pair, tiles, u0, d0, gu, gd in ((0, FF1, U_UP1, U_DN1, G_UP1, G_DN1),
                                                          (FF1, FF2, U_UP2, U_DN2, G_UP2, G_DN2)):
                    with dve.Fori(0, tiles // 2) as u:
                        links = [count[0]]

                        def loop_link(ins):
                            links[0] += 1
                            ins.then_inc(v_chain, 1)
                            dve.wait_ge(v_chain, V_CHAIN * l + 8 * u + links[0])

                        for j in range(4):
                            xp, o = xpad[j % 2], cv[j]
                            sum_parts(gu + j, u0 + j, xp[:, 3:3 + SEQ], 4 * u)
                            dve.wait_ge(gemm_evac, GROUPS * l + 4 * u + (BANKS + gu + j + 1))
                            dve.wait_ge(prod_done, FF_TILES * l + 2 * u + (first_pair + j // 2 + 1))
                            tile = 2 * first_pair + j
                            w = [col[:, bass.ds(12 * u + (C_FW + 3 * tile + k), 1)] for k in range(3)]
                            b = col[:, bass.ds(4 * u + (C_FB + tile), 1)]
                            loop_link(v.tensor_scalar(o[:, :], xp[:, 3:3 + SEQ], w[2], b, ALU.mult, ALU.add))
                            loop_link(v.scalar_tensor_tensor(o[:, :], xp[:, 1:1 + SEQ], w[0], o[:, :],
                                                             ALU.mult, ALU.add))
                            v.scalar_tensor_tensor(o[:, :], xp[:, 2:2 + SEQ], w[1], o[:, :], ALU.mult, ALU.add
                                                   ).then_inc(conv_done, 1)
                            lo(u0 + j + AHEAD, u, 4)
                        assert links[0] - count[0] == 8
                    count[0] += 8 * (tiles // 2)
                    if first_pair == 0:
                        with dve.Fori(0, 2) as u:
                            for cc in range(2):
                                for r in range(6):
                                    lo(d0 + 6 * cc + r + AHEAD, u, 12)
                                for half in range(HALVES):
                                    out_rows(gd + 2 * cc + half, d0 + 6 * cc + 5, cc, half, False, 12 * u, 2 * CHUNK * u)
                    else:
                        for c in range(CHUNKS):
                            for r in range(5):
                                if c and r == 1:
                                    rows_and_stats(gd + 2 * c - 2, d0 + 5 * c - 1, c - 1)
                                if d0 + 5 * c + r + AHEAD < UNITS:
                                    lo(d0 + 5 * c + r + AHEAD)
                link(rows_and_stats(G_DN2 + 6, UNITS - 1, 3))
                layer_norm(1)
                assert count[0] - start[0] < V_CHAIN, count
                dve.sem_inc(v_chain, V_CHAIN - (count[0] - start[0]))

        @block.tensor
        def _(pe):
            t = nc.tensor

            def mm_(out_ap, lhsT, rhs, start, stop):
                return t.matmul(out_ap, lhsT, rhs, start=start, stop=stop, skip_group_check=True)

            pe.sem_inc(unit_used, RING)

            with pe.Fori(0, DEPTH) as l:

                def weights_of(i, u=None, step=0):
                    pe.wait_ge(lo_done, UNITS * l + (0 if u is None else step * u) + i + 1)
                    return split[i % RING]

                def bank_free(g, more=0):
                    pe.wait_ge(gemm_evac, GROUPS * l + more + g + 1)
                    return gp[g % BANKS]

                def a_unit(i, lhs, kts, g, first, last, ready=None, u=None, step=0, more=0):
                    w = weights_of(i, u, step)
                    banks = [bank_free(g + half, more) if first else gp[(g + half) % BANKS]
                             for half in range(HALVES)]
                    for n, kt in enumerate(kts):
                        if ready is not None:
                            ready(kt)
                        w_hi, w_lo = (w[:, part, CHUNK * n:CHUNK * (n + 1)] for part in range(2))
                        for half in range(HALVES):
                            a_hi = lhs[:, kt, P * half:P * (half + 1)]
                            a_lo = lhs[:, kt, SEQ + P * half:SEQ + P * (half + 1)]
                            mm_(banks[half][:, :], a_hi, w_hi, first and n == 0, False)
                            mm_(banks[half][:, :], a_hi, w_lo, False, False)
                            ins = mm_(banks[half][:, :], a_lo, w_hi, False, last and n == len(kts) - 1)
                    ins.then_inc(unit_used, 1)

                def b_unit(i, g, u=None, step=0, more=0):
                    w = weights_of(i, u, step)
                    bank = bank_free(g, more)
                    for kt in range(KT):
                        mm_(bank[:, :], w[:, 0, P * kt:P * (kt + 1)], hT[:, kt, :], kt == 0, False)
                        ins = mm_(bank[:, 0:SEQ], w[:, 1, P * kt:P * (kt + 1)], hT[:, kt, 0:SEQ], False, kt == KT - 1)
                    ins.then_inc(unit_used, 1)

                def norm_transposes(which):
                    for kt in range(KT):
                        if kt % 4 == 0:
                            pe.wait_ge(ln_norm, 2 * CHUNKS * l + CHUNKS * which + kt // 4 + 1)
                        if kt >= 4:
                            pe.wait_ge(ln_aff, 2 * KT * l + KT * which + kt - 3)
                        for half in range(HALVES):
                            ins = t.transpose(xq[kt % 4][:, P * half:P * (half + 1)],
                                              acc[:, half, P * kt:P * (kt + 1)], ident)
                        ins.then_inc(ln_mm, 1)

                def new_hT(n):
                    return lambda kt: pe.wait_ge(hT_ready, 2 * KT * l + KT * n + kt + 1)

                if l is not None:
                    pe.wait_ge(start_in, 48)
                for c in range(2):
                    for r in range(4):
                        a_unit(U_V + 4 * c + r, hT, range(4 * r, 4 * r + 4), G_V + 2 * c, r == 0, r == 3,
                               new_hT(0) if c == 0 else None)
                pe.wait_ge(wdt_ready, l + 1)
                for half in range(HALVES):
                    for kt in range(KT):
                        mm_(xq[0][:, 32 * half:32 * half + 32], hT[:, kt, P * half:P * (half + 1)], wdt_s[:, kt, :],
                            kt == 0, False)
                        ins = mm_(xq[0][:, 32 * half:32 * half + 16], hT[:, kt, SEQ + P * half:SEQ + P * (half + 1)],
                                  wdt_s[:, kt, 0:16], False, kt == KT - 1)
                ins.then_inc(dt_mm, 1)

                for j in range(XBC_TILES):
                    if j == 2:
                        pe.wait_ge(da_ready, 2 * l + 2)
                        da = [dtx[:, 11, 16 * half:16 * half + 16] for half in range(HALVES)]
                        mm_(xq[1][:, 0:16], tri, da[0], True, True)
                        mm_(xq[1][:, 16:32], ones, da[0], True, False)
                        mm_(xq[1][:, 16:32], tri, da[1], False, True).then_inc(acs_mm, 1)
                    if j == 5:
                        pe.wait_ge(acs_ready, l + 1)
                        for half in range(HALVES):
                            ins = t.transpose(xq[2][0:16, P * half:P * (half + 1)], acs[:, half, :], ident)
                        ins.then_inc(acsT_mm, 1)
                    b_unit(U_XBC + j, G_XBC + j)

                for j in range(Z_TILES):
                    if j in (1, 2):
                        g = j - 1
                        if g == 0:
                            pe.wait_ge(xsilu_done, XBC_TILES * l + XBC_TILES)
                            pe.wait_ge(acsT_ready, l + 1)
                        mm_(xq[j][:, 0:256], bcT[:, g, 0:P], bcT[:, 2 + g, :], True, True)
                        mm_(xq[j][:, 256:384], bcT[:, g, P:SEQ], bcT[:, 2 + g, P:SEQ], True, True).then_inc(cb_mm, 1)
                    if 3 <= j < 7:
                        half, q = (j - 3) // 2, (j - 3) % 2
                        if j > 3:
                            pe.wait_ge(xdt_ready, 4 * l + j - 3)
                        for n in range(4):
                            ins = t.transpose(xq[3][:, P * n:P * (n + 1)], xbT[:, 4 * q + n, P * half:P * (half + 1)],
                                              ident)
                        ins.then_inc(xt_mm, 1)
                    b_unit(U_Z + j, G_Z + j)

                def decay_row(h):
                    pe.wait_ge(seg_done, SSD_HEADS * l + h) if h else pe.wait_ge(acsT_ready, l + 1)
                    mm_(xq[0][:, 0:SEQ], ident[0:16, h:h + 1].to_broadcast([16, P]), acsT[:, :], True, True
                        ).then_inc(row_mm, 1)

                def y_head(h):
                    if h == 0:
                        pe.wait_ge(cb_ready, SSD_GROUPS * l + 2)
                        pe.wait_ge(xdt_ready, 4 * l + 4)
                    elif h % 2 == 0:
                        pe.wait_ge(y_read, X_TILES * l + h // 2)
                    pe.wait_ge(m_done, SSD_HEADS * l + h + 1)
                    p0 = SSD_HD * (h % 2)
                    mm_(xq[1][p0:p0 + SSD_HD, 0:SEQ], xdt[:, 0, SSD_HD * h:SSD_HD * (h + 1)], mm[h % 2][:, 0:256],
                        True, False)
                    mm_(xq[1][p0:p0 + SSD_HD, P:SEQ], xdt[:, 1, SSD_HD * h:SSD_HD * (h + 1)], mm[h % 2][:, 256:384],
                        False, True).then_inc(y_mm, 1)

                def y_sums(j):
                    if j == 4:
                        pe.wait_ge(yrms_read, SSD_GROUPS * l + 1)
                    pe.wait_ge(ysq_done, X_TILES * l + j + 1)
                    mm_(xq[2][:, 0:SEQ], ones, sq[j % 2][:, :], j % 4 == 0, j % 4 == 3).then_inc(yrms_mm, 1)

                def qk_transposes(c, b):
                    pe.wait_ge(rope_done, 8 * l + 2 * c + 2)
                    if c or b:
                        pe.wait_ge(qkT_ready, 8 * l + 2 * c + b)
                    for n in range(2):
                        for half in range(HALVES):
                            ins = t.transpose(xq[3][:, SEQ * n + P * half:SEQ * n + P * (half + 1)],
                                              qk_tok[c % 2][:, half, HD * (2 * b + n):HD * (2 * b + n + 1)], ident)
                    ins.then_inc(qkT_mm, 1)

                for h in range(SSD_HEADS):
                    if h >= 2:
                        y_head(h - 2)
                    decay_row(h)
                    if h >= 4 and h % 2 == 0:
                        y_sums(h // 2 - 2)
                    if h >= 6 and h % 4 >= 2:
                        qk_transposes((h - 6) // 4, h % 4 - 2)
                    a_unit(U_QK + h, hT, range(4 * (h % 4), 4 * (h % 4) + 4), G_QK + 2 * (h // 4), h % 4 == 0,
                           h % 4 == 3)
                y_head(SSD_HEADS - 2)
                y_head(SSD_HEADS - 1)
                qk_transposes(3, 0)
                y_sums(X_TILES - 2)
                y_sums(X_TILES - 1)

                def scores(h):
                    if h == 0:
                        pe.wait_ge(seg_done, SSD_HEADS * l + SSD_HEADS)
                    else:
                        pe.wait_ge(sc_read, HEADS * l + h)
                    if h == 0:
                        pe.wait_ge(qkT_ready, 8 * l + 4)
                    elif h == 4:
                        pe.wait_ge(qkT_ready, 8 * l + 8)
                    mm_(xq[0][:, 0:128], qT[:, h, 0:P], kT[:, h, 0:P], True, True)
                    mm_(xq[0][:, 128:384], qT[:, h, P:SEQ], kT[:, h, :], True, True).then_inc(sc_mm, 1)

                def prob_transposes(h):
                    if h:
                        pe.wait_ge(prT_ready, HEADS * l + h)
                    pe.wait_ge(prob_done, HEADS * l + h + 1)
                    for n in range(3):
                        ins = t.transpose(xq[1][:, P * n:P * (n + 1)], sco[h % 2][:, P * n:P * (n + 1)], ident)
                    ins.then_inc(prT_mm, 1)

                def values(h):
                    if h:
                        pe.wait_ge(osq_done, HEADS * l + h)
                    else:
                        pe.wait_ge(yrms_read, SSD_GROUPS * l + 2)
                    pe.wait_ge(prT_ready, HEADS * l + h + 1)
                    mm_(xq[2][:, 0:SEQ], v_tok[:, 0, HD * h:HD * (h + 1)], prT[h % 2][:, 0:256], True, False)
                    mm_(xq[2][:, P:SEQ], v_tok[:, 1, HD * h:HD * (h + 1)], prT[h % 2][:, 256:384], False, True
                        ).then_inc(o_mm, 1)

                def out_sums(h):
                    if h == 0:
                        pe.wait_ge(qkT_ready, 8 * l + 8)
                    pe.wait_ge(osq_done, HEADS * l + h + 1)
                    mm_(xq[3][:, 0:SEQ], ones, sq[h % 2][:, :], h == 0, h == HEADS - 1).then_inc(orms_mm, 1)

                for h in range(HEADS):
                    if h >= 2:
                        values(h - 2)
                    if h >= 1:
                        prob_transposes(h - 1)
                    scores(h)
                    if h == 0:
                        qk_transposes(3, 1)
                    if h >= 3:
                        out_sums(h - 3)
                    if h < 2:
                        pe.wait_ge(mix_ready, 4 * l + h + 1)
                    a_unit(U_WS + h, hT, range(8 + 4 * (h % 2), 12 + 4 * (h % 2)), G_WS + 2 * (h // 2), h % 2 == 0,
                           h % 2 == 1)
                values(HEADS - 2)
                prob_transposes(HEADS - 1)
                out_sums(HEADS - 3)
                values(HEADS - 1)
                out_sums(HEADS - 2)
                out_sums(HEADS - 1)
                for r in range(8):
                    if r < 2:
                        pe.wait_ge(mix_ready, 4 * l + r + 3)
                    a_unit(U_WA + r, hT, range(4 * (r % 2), 4 * (r % 2) + 4), G_WA + 2 * (r // 2), r % 2 == 0,
                           r % 2 == 1)
                norm_transposes(0)

                for c in range(CHUNKS):
                    for r in range(4):
                        a_unit(U_GP + 5 * c + r, hT, range(4 * r, 4 * r + 4), G_GP + 4 * c, r == 0, r == 3,
                               new_hT(1) if c == 0 else None)
                    if c == 0:
                        pe.wait_ge(p_ready, l + 1)
                    a_unit(U_GP + 5 * c + 4, p_s, range(2), G_GP + 4 * c + 2, True, True)

                for first, tiles, u0, d0, gu, gd in ((0, FF1, U_UP1, U_DN1, G_UP1, G_DN1),
                                                     (FF1, FF2, U_UP2, U_DN2, G_UP2, G_DN2)):
                    with pe.Fori(0, tiles // 2) as u:
                        for j in range(4):
                            b_unit(u0 + j, gu + j, u, 4, 4 * u)

                    def down(i, c, r, deep, u=None, ready=False):
                        kts = range(4 * r, 4 * r + 4)
                        more, gmore = (0, 0) if u is None else (12, 4 * u)
                        if ready:
                            pe.wait_ge(ff_ready, FF_TILES * l + first + 4 * r + 4)
                        a_unit(i, ffT, kts, gd + 2 * c, r == 0, r == deep - 1, None, u, more, gmore)

                    if first == 0:
                        with pe.Fori(0, 2) as u:
                            for cc in range(2):
                                for r in range(6):
                                    down(d0 + 6 * cc + r, cc, r, 6, u, cc == 0)
                    else:
                        for c in range(CHUNKS):
                            for r in range(5):
                                down(d0 + 5 * c + r, c, r, 5, None, c == 0)
                norm_transposes(1)


def _tiles_b(w, cols):
    k, n = w.shape
    return w.reshape(k // P, P, n // P, P).transpose(2, 1, 0, 3).reshape(n // P, P, -1)[:cols]


def _tiles_a(w, deep=4):
    k, n = w.shape
    return w.reshape(k // (P * deep), deep, P, n // CHUNK, CHUNK).transpose(3, 0, 2, 1, 4).reshape(-1, P, deep * CHUNK)


def _column(v):
    return v.reshape(-1, P).T


def kernel(**inputs):
    import concourse.bacc as _bacc
    from concourse.bass_utils import run_bass_kernel_spmd as _run

    a = {k: np.asarray(v) for k, v in inputs.items()}
    weights = np.zeros((DEPTH * UNITS, P, UNIT), np.float32)
    cols = np.zeros((DEPTH, P, COLS), np.float32)
    rows = np.zeros((DEPTH, P, 32), np.float32)
    Q, K, V, Z, XBC, DT = 0, 1024, 2048, 3072, 4096, 5632
    xbc_order = [8, 9, 10, 11, *range(8)]
    for l in range(DEPTH):
        w = weights[l * UNITS:(l + 1) * UNITS]
        w_in = a["w_in"][l]
        w[U_V:U_XBC] = _tiles_a(w_in[:, V:Z])
        w[U_XBC:U_Z] = _tiles_b(w_in[:, XBC:DT], 12)[xbc_order]
        w[U_Z:U_QK] = _tiles_b(w_in[:, Z:XBC], 8)
        q, k = _tiles_a(w_in[:, Q:K]), _tiles_a(w_in[:, K:V])
        for c in range(2):
            w[U_QK + 8 * c:U_QK + 8 * c + 4] = q[4 * c:4 * c + 4]
            w[U_QK + 8 * c + 4:U_QK + 8 * c + 8] = k[4 * c:4 * c + 4]
        w[U_WS:U_WA] = _tiles_a(a["w_out"][l][ATTN_WIDTH:])
        w[U_WA:U_GP] = _tiles_a(a["w_out"][l][:ATTN_WIDTH])
        gate, emb = _tiles_a(a["w_pe_gate"][l]), _tiles_a(a["w_pe_proj"][l], 2)
        for c in range(CHUNKS):
            w[U_GP + 5 * c:U_GP + 5 * c + 4] = gate[4 * c:4 * c + 4]
            w[U_GP + 5 * c + 4, :, 0:2 * CHUNK] = emb[c]
        up = _tiles_b(a["w_up"][l], 2 * FF_TILES).reshape(2, FF_TILES, P, UNIT).swapaxes(0, 1)
        w[U_UP1:U_DN1] = up[:FF1].reshape(-1, P, UNIT)
        w[U_UP2:U_DN2] = up[FF1:].reshape(-1, P, UNIT)
        w[U_DN1:U_UP2] = _tiles_a(a["w_down"][l][:FF1 * P])
        w[U_DN2:UNITS] = _tiles_a(a["w_down"][l][FF1 * P:])

        c = cols[l]
        conv_w = a["ssd_conv_w"][l].reshape(4, XBC_TILES, P)[:, xbc_order]
        c[:, C_XW:C_XB] = conv_w.transpose(2, 1, 0).reshape(P, -1)
        c[:, C_XB:C_SN] = _column(a["ssd_conv_b"][l])[:, xbc_order]
        c[:, C_SN:C_AN] = _column(a["ssd_norm_g"][l])
        c[:, C_AN:C_D] = _column(a["attn_norm_g"][l])
        c[:, C_D:C_L1G] = _column(np.repeat(a["ssd_d"][l], SSD_HD))
        for at, name in ((C_L1G, "ln1_g"), (C_L1B, "ln1_b"), (C_L2G, "ln2_g"), (C_L2B, "ln2_b")):
            c[:, at:at + KT] = _column(a[name][l])
        ffn_w = a["ffn_conv_w"][l].reshape(3, 2, FF_TILES, P)
        c[:, C_FW:C_FB] = ffn_w.transpose(3, 2, 1, 0).reshape(P, -1)
        c[:, C_FB:COLS] = a["ffn_conv_b"][l].reshape(2, FF_TILES, P).transpose(2, 1, 0).reshape(P, -1)
        rows[l, :, 0:16] = a["ssd_dt_bias"][l]
        rows[l, :, 16:32] = a["ssd_a_log"][l]

    consts = np.zeros((P, CONSTS), np.float32)
    i = np.arange(P)
    consts[:, K_ID:K_ID + P] = np.eye(P)
    consts[:, K_ONE:K_ONE + P] = 1.0
    consts[:, K_TRI:K_TRI + P] = i[:, None] <= i[None, :]
    hidden = np.float32(-3e38)
    query_key = np.where(i[None, :] <= i[:, None], np.float32(0), hidden)
    consts[:, K_AMASK:K_AMASK + P] = query_key
    consts[:, K_AMASK + 2 * P:K_AMASK + 3 * P] = query_key
    consts[:, K_SMASK:K_SMASK + P] = query_key.T
    consts[:, K_FREQ:K_FREQ + 16] = np.float32(1.0) / (np.float32(500000.0) ** (np.arange(0, 32, 2, dtype=np.float32)
                                                                                   / np.float32(32)))
    x = a["x"][0]
    arrays = {
        "x_tok": x.reshape(HALVES, P, D_MODEL).transpose(1, 0, 2),
        "x_T": x.T.reshape(KT, P, SEQ).transpose(1, 0, 2),
        "p_T": a["p"][:, 0].transpose(0, 2, 1).reshape(DEPTH, 2, P, SEQ).transpose(0, 2, 1, 3),
        "pos": a["positions"].reshape(HALVES, P).T,
        "weights": weights,
        "w_dt": a["w_in"][:, :, DT:].reshape(DEPTH, KT, P, 16).transpose(0, 2, 1, 3),
        "cols": cols,
        "rows": rows,
        "norm_rows": np.stack([a["ln1_g"], a["ln1_b"], a["ln2_g"], a["ln2_b"]], 1).reshape(2 * DEPTH, 2, D_MODEL),
        "consts": consts,
    }
    nc = _bacc.Bacc("TRN2", target_bir_lowering=False, num_devices=1)
    args = []
    for name, v in arrays.items():
        arrays[name] = v = np.ascontiguousarray(v)
        args.append(nc.dram_tensor(name, v.shape, mybir.dt.from_np(v.dtype), kind="ExternalInput").ap())
    out = nc.dram_tensor("out", (P, HALVES, D_MODEL), F32, kind="ExternalOutput").ap()
    build(nc, *args, out)
    r = _run(nc, [arrays], core_ids=[0])
    return r.results[0]["out"].transpose(1, 0, 2).reshape(1, SEQ, D_MODEL)
```

```python
from contextlib import ExitStack

import numpy as np

import concourse.bass as bass
from concourse import mybir

F32 = mybir.dt.float32
F32R = mybir.dt.float32r
I32 = mybir.dt.int32
ACT = mybir.ActivationFunctionType
ALU = mybir.AluOpType
AX_X = mybir.AxisListType.X

P = 128
D_MODEL, SEQ, DEPTH, PE_DIM = 2048, 256, 2, 256
HALVES = SEQ // P
KT = D_MODEL // P
CHUNK = 512
CHUNKS = D_MODEL // CHUNK
HEADS, HD = 8, 128
ATTN_WIDTH = HEADS * HD
SSD_HEADS, SSD_HD, SSD_GROUPS = 16, 64, 2
XBC_TILES, X_TILES, Z_TILES = 12, 8, 8
D_FF = 5632
FF_TILES = D_FF // P
FF1 = 24
FF2 = FF_TILES - FF1
ALPHA = float((2 * DEPTH) ** 0.25)
LN_EPS, RMS_EPS = 1e-5, 1e-6
SCALE = HD ** -0.5
UNIT = 2048

U_V = 0
U_XBC = U_V + 8
U_Z = U_XBC + XBC_TILES
U_QK = U_Z + Z_TILES
U_WS = U_QK + 16
U_PA = U_WS + 8
U_WA = U_PA + 2
U_PB = U_WA + 8
U_GATE = U_PB + 2
U_UP1 = U_GATE + 4 * CHUNKS
U_DN1 = U_UP1 + 2 * FF1
U_UP2 = U_DN1 + FF1 // 4 * CHUNKS
U_DN2 = U_UP2 + 2 * FF2
UNITS = U_DN2 + FF2 // 4 * CHUNKS
G_V = 0
G_XBC = G_V + 4
G_Z = G_XBC + XBC_TILES
G_QK = G_Z + Z_TILES
G_WS = G_QK + 8
G_PA = G_WS + 8
G_WA = G_PA + 4
G_PB = G_WA + 8
G_GATE = G_PB + 4
G_UP1 = G_GATE + 2 * CHUNKS
G_DN1 = G_UP1 + 2 * FF1
G_UP2 = G_DN1 + 2 * CHUNKS
G_DN2 = G_UP2 + 2 * FF2
GROUPS = G_DN2 + 2 * CHUNKS
RAW, RING, BANKS = 2, 4, 4
AHEAD = RING - 1
WS_ORDER = [(0, 0), (1, 0), (0, 1), (1, 1), (2, 0), (2, 1), (3, 0), (3, 1)]
MIXES = 2 + HEADS // 2
assert UNITS % RING == 0 and GROUPS % BANKS == 0

C_XW, C_XB, C_SN, C_AN, C_D = 0, 48, 60, 68, 76
C_L1G, C_L1B = 84, 100
C_FW, C_FB = 116, 116 + 3 * 2 * FF_TILES
COLS = C_FB + 2 * FF_TILES
K_ID, K_ONE, K_TRI, K_AMASK, K_SMASK, K_FREQ, K_COL = 0, 128, 256, 384, 768, 1024, 1040
CONSTS = 1043
TWO_PI_PARTS = []
_rest = 2 * np.pi
for _bits in (2 ** -2, 2 ** -9, 2 ** -15, 2 ** -21):
    _part = float(np.floor(_rest / _bits) * _bits)
    TWO_PI_PARTS.append(_part)
    _rest -= _part
TWO_PI_PARTS.append(float(_rest))
ROUND = 1.5 * 2.0 ** 23
V_CHAIN = 1024
G_CHAIN = 256


def build(nc, x_tok, pT, pos, weights, wdt, cols, cols_in, rows, gb, consts, out):
    with ExitStack() as ctx:
        ctx.enter_context(nc.allow_non_contiguous_dma(reason="small parameter rows"))
        place = [(nc.sbuf_base + 31) // 32 * 32]

        def keep(name, shape, dt=F32):
            size = int(np.prod(shape[1:])) * 4
            t = nc.alloc_sbuf_tensor_at(name, shape, dt, offset=place[0])
            place[0] += (size + 31) // 32 * 32
            return t

        hT = keep("hT", [P, KT, 2 * SEQ], F32R)
        acc = keep("acc", [P, HALVES, D_MODEL])
        raw = [keep(f"raw{i}", [P, UNIT]) for i in range(RAW)]
        split = [keep(f"split{i}", [P, 2, UNIT], F32R) for i in range(RING)]
        cst = keep("cst", [P, CONSTS])
        col = keep("col", [P, COLS])
        col_in = keep("col_in", [P, 2 * KT])
        row = keep("row", [P, 32])
        cos = keep("cos", [P, HALVES, 32])
        sin = keep("sin", [P, HALVES, 32])
        dtx = keep("dtx", [P, 12, 32])
        angle = dtx[:, 8:10, :]
        acs = keep("acs", [P, HALVES, 16])
        acsT = keep("acsT", [48, SEQ], F32R)
        pick = keep("pick", [48, 16], F32R)
        stat = keep("stat", [P, 2, 8])
        bn = keep("bn", [P, HALVES, 6 * CHUNKS])
        ln = keep("ln", [P, HALVES, 6])
        xpad = [keep(f"xpad{i}", [P, 3 + SEQ]) for i in range(2)]
        region = place[0]

        def at(name, kib, shape, dt=F32):
            off = region + int(kib * 1024)
            assert off + int(np.prod(shape[1:])) * 4 <= nc.sbuf_usable_end, name
            return nc.alloc_sbuf_tensor_at(name, shape, dt, offset=off)

        xbT = at("xbT", 0, [P, X_TILES, SEQ])
        bcT = at("bcT", 8, [P, 4, SEQ])
        zs = at("zs", 12, [P, Z_TILES, SEQ])
        xdt = at("xdt", 20, [P, HALVES, 1024])
        cb = at("cb", 28, [P, SSD_GROUPS, 384])
        seg = [at(f"seg{i}", 31 + 1.5 * i, [P, 384]) for i in range(2)]
        mm = [at(f"mm{i}", 34 + 1.5 * i, [P, 384]) for i in range(2)]
        v_tok = at("v_tok", 37, [P, HALVES, ATTN_WIDTH])
        qk_tok = [at("qk_tok0", 8, [P, HALVES, CHUNK]), at("qk_tok1", 45, [P, HALVES, CHUNK])]
        qT = at("qT", 49, [P, HEADS, SEQ])
        kT = at("kT", 57, [P, HEADS, SEQ])
        sq = [at(f"sq{i}", 65 + i, [P, SEQ]) for i in range(2)]
        rms_s = at("rms_s", 67, [P, SEQ])
        rope = xpad[0][:, 3:3 + SEQ].rearrange("p (a n) -> p a n", a=2)
        tmp = xpad[1][:, 3:3 + SEQ]
        conv = [at(f"conv{i}", 49 + i, [P, SEQ]) for i in range(2)]
        oT = at("oT", 0, [P, HEADS, SEQ])
        sco = [at(f"sco{i}", 31 + 1.5 * i, [P, 384]) for i in range(2)]
        prT = [at(f"prT{i}", 34 + 1.5 * i, [P, 384]) for i in range(2)]
        wdt_raw = at("wdt_raw", 57, [P, KT, 16])
        wdt_s = at("wdt_s", 58, [P, KT, 32], F32R)
        lnf = [at(f"lnf{i}", 65 + i, [P, SEQ]) for i in range(2)]
        gbt = at("gbt", 61, [P, 2, CHUNK])
        emb = at("emb", 12, [P, HALVES, D_MODEL])
        sig = [at(f"sig{i}", 2 * i, [P, CHUNK]) for i in range(2)]
        gated = [at(f"gated{i}", 4 + 2 * i, [P, CHUNK]) for i in range(2)]
        p_raw = at("p_raw", 28, [P, 2, SEQ])
        p_s = at("p_s", 8, [P, 2, 2 * SEQ], F32R)
        ffT = at("ffT", 0, [P, FF1, 2 * SEQ], F32R)
        cv = [at(f"cv{i}", 48 + i, [P, SEQ]) for i in range(4)]
        gs = [at(f"gs{i}", 52 + i, [P, SEQ]) for i in range(2)]
        prod = [at(f"prod{i}", 54 + i, [P, SEQ]) for i in range(2)]
        ang = at("ang", 20, [P, 6, 32])
        posi = at("posi", 21, [P, HALVES], I32)
        gb_last = at("gb_last", 48, [P, 2, D_MODEL])

        gp = [ctx.enter_context(nc.psum_tensor(f"gp{i}", [P, 512], F32)) for i in range(BANKS)]
        xq = [ctx.enter_context(nc.psum_tensor(f"xq{i}", [P, 512], F32)) for i in range(4)]

        ident, ones, tri = cst[:, K_ID:K_ID + P], cst[:, K_ONE:K_ONE + P], cst[:, K_TRI:K_TRI + P]
        amask = cst[:, K_AMASK:K_AMASK + 384]
        smask = cst[:, K_SMASK:K_SMASK + 256]

        def sem(name):
            return ctx.enter_context(nc.semaphore(name))

        raw_in = [sem(f"raw_in{i}") for i in range(RAW)]
        x_in = [sem(f"x_in{c}") for c in range(CHUNKS)]
        pos_in, start_in, par_in, col_in_in, p_in, gb_in, gbl_in, out_in = (sem(n) for n in (
            "pos_in", "start_in", "par_in", "col_in_in", "p_in", "gb_in", "gbl_in", "out_in"))
        hi_done, lo_done, unit_used = sem("hi_done"), sem("lo_done"), sem("unit_used")
        gemm_evac = sem("gemm_evac")
        hT_ready, mixhi_done, mix_ready = sem("hT_ready"), sem("mixhi_done"), sem("mix_ready")
        v_chain, g_chain = sem("v_chain"), sem("g_chain")
        ang_done, trig_done = sem("ang_done"), sem("trig_done")
        wdt_hi, wdt_ready, dt_mm, dt_pre, dt_exp, a_exp = (sem(n) for n in (
            "wdt_hi", "wdt_ready", "dt_mm", "dt_pre", "dt_exp", "a_exp"))
        da_ready, acs_mm, acs_ready, acsT_mm, acsT_ready = (sem(n) for n in (
            "da_ready", "acs_mm", "acs_ready", "acsT_mm", "acsT_ready"))
        xconv_done, xsilu_done, zsilu_done, cb_mm, cb_ready, xt_mm, xdt_ready = (sem(n) for n in (
            "xconv_done", "xsilu_done", "zsilu_done", "cb_mm", "cb_ready", "xt_mm", "xdt_ready"))
        row_mm, seg_done, segexp_done, m_done, y_mm, y_read = (sem(n) for n in (
            "row_mm", "seg_done", "segexp_done", "m_done", "y_mm", "y_read"))
        yg_done, ysq_done, yrms_mm, yrms_read, yn_done = (sem(n) for n in (
            "yg_done", "ysq_done", "yrms_mm", "yrms_read", "yn_done"))
        orms_read, root_done, spread_mm = sem("orms_read"), sem("root_done"), sem("spread_mm")
        rope_done, qkT_mm, qkT_ready = sem("rope_done"), sem("qkT_mm"), sem("qkT_ready")
        sc_mm, sc_read, max_done, exp_done, prob_done = (sem(n) for n in (
            "sc_mm", "sc_read", "max_done", "exp_done", "prob_done"))
        prT_mm, prT_ready, o_mm, osq_done, orms_mm, on_done = (sem(n) for n in (
            "prT_mm", "prT_ready", "o_mm", "osq_done", "orms_mm", "on_done"))
        ln_norm, ln_mm, ln_aff, ln_res = (sem(n) for n in ("ln_norm", "ln_mm", "ln_aff", "ln_res"))
        p_hi, p_ready, gate_read = sem("p_hi"), sem("p_ready"), sem("gate_read")
        col_in_set = sem("col_in_set")
        half_done = sem("half_done")
        factors_ready, fin_norm, fin_done = sem("factors_ready"), sem("fin_norm"), sem("fin_done")
        conv_done, silu_done, prod_done, ffhi_done, ff_ready = (sem(n) for n in (
            "conv_done", "silu_done", "prod_done", "ffhi_done", "ff_ready"))

        block = ctx.enter_context(nc.Block())

        @block.sync
        def _(sp):
            def load(n, slot):
                sp.dma_start(raw[slot][:, :], weights[n]).then_inc(raw_in[slot], 16)

            def load_x(c):
                sp.dma_start(acc[:, :, c * CHUNK:(c + 1) * CHUNK], x_tok[:, :, c * CHUNK:(c + 1) * CHUNK]
                             ).then_inc(x_in[c], 16)

            load(0, 0)
            load_x(0)
            sp.dma_start(posi[:, :], pos).then_inc(pos_in, 16)
            load_x(1)
            load(1, 1)
            load_x(2)
            load_x(3)
            with sp.Fori(1, DEPTH * UNITS // RAW) as u:
                for slot in range(RAW):
                    sp.wait_ge(lo_done, RAW * u + slot - RAW + 1)
                    sp.dma_start(raw[slot][:, :], weights[bass.ds(RAW * u + slot, 1)].rearrange("a p n -> p (a n)")
                                 ).then_inc(raw_in[slot], 16)
            sp.wait_ge(lo_done, DEPTH * UNITS - RAW + 1)
            load(0, 0)
            sp.wait_ge(ln_res, 1 + DEPTH * 4 * CHUNKS + HALVES)
            sp.dma_start(out[:, :, 0:CHUNK], acc[:, :, 0:CHUNK]).then_inc(out_in, 16)
            for c in range(1, CHUNKS):
                sp.wait_ge(fin_done, 2 * c)
                sp.dma_start(out[:, :, c * CHUNK:(c + 1) * CHUNK], acc[:, :, c * CHUNK:(c + 1) * CHUNK]
                             ).then_inc(out_in, 16)
            sp.wait_ge(out_in, 16 * CHUNKS)

        @block.gpsimd
        def _(pool):
            g = nc.gpsimd
            g.dma_start(cst[:, :], consts).then_inc(start_in, 16)

            pool.sem_inc(prod_done, 2)
            pool.sem_inc(ln_res, 1)

            with pool.Fori(0, DEPTH) as l:
                count = [0]

                def link(ins):
                    count[0] += 1
                    ins.then_inc(g_chain, 1)
                    pool.wait_ge(g_chain, G_CHAIN * l + count[0])

                pool.wait_ge(gemm_evac, GROUPS * l + BANKS)
                g.dma_start(col[:, :], cols[bass.ds(l, 1)].rearrange("a p n -> p (a n)")).then_inc(par_in, 16)
                g.dma_start(row[:, :], rows[bass.ds(l, 1)].rearrange("a p n -> p (a n)")).then_inc(par_in, 16)
                g.dma_start(wdt_raw[:, :, :], wdt[bass.ds(l, 1)].rearrange("a p k n -> p (a k) n")).then_inc(par_in, 16)

                def residual(which):
                    for c in range(CHUNKS):
                        if c:
                            pool.wait_ge(ln_res, 1 + (2 * l + which) * 2 * CHUNKS + 2 * c)
                        elif which:
                            pool.wait_ge(sc_mm, HEADS * l + HEADS)
                        g.dma_start(gbt[:, :, :], gb[bass.ds(2 * l + which, 1), :, c * CHUNK:(c + 1) * CHUNK]
                                    .to_broadcast([P, 2, CHUNK])).then_inc(gb_in, 16)
                        if c == 0:
                            pool.wait_ge(ln_mm, 2 * KT * l + KT * which + KT)
                        pool.wait_ge(gb_in, 16 * ((2 * l + which) * CHUNKS + c + 1))
                        for half in range(HALVES):
                            t = acc[:, half, c * CHUNK:(c + 1) * CHUNK]
                            link(g.tensor_tensor(t, t, gbt[:, 0, :], ALU.mult))
                            g.tensor_tensor(t, t, gbt[:, 1, :], ALU.add).then_inc(ln_res, 1)

                residual(0)

                def ssd_product(h):
                    pool.wait_ge(segexp_done, SSD_HEADS * l + h + 1)
                    if h == 0:
                        pool.wait_ge(cb_ready, SSD_GROUPS * l + 2)
                    if h >= 2:
                        pool.wait_ge(y_mm, SSD_HEADS * l + h - 1)
                    g.tensor_tensor(mm[h % 2][:, :], seg[h % 2][:, :], cb[:, h // 8, :], ALU.mult).then_inc(m_done, 1)

                def rotate(c):
                    if c == 0:
                        pool.wait_ge(trig_done, l + 1)
                    for half in range(HALVES):
                        pool.wait_ge(gemm_evac, BANKS + GROUPS * l + G_QK + 2 * c + half + 1)
                        if c or half:
                            pool.wait_ge(rope_done, 8 * l + 2 * c + half)
                        t = qk_tok[c % 2][:, half, :].rearrange("p (h d) -> p h d", d=HD)
                        cs = cos[:, half, :].unsqueeze(1).to_broadcast([P, 4, 32])
                        sn = sin[:, half, :].unsqueeze(1).to_broadcast([P, 4, 32])
                        a = rope[:, 0, :].rearrange("p (h d) -> p h d", d=32)
                        b = rope[:, 1, :].rearrange("p (h d) -> p h d", d=32)
                        g.tensor_tensor(a, t[:, :, 0:32], cs, ALU.mult)
                        g.tensor_tensor(b[:, :, 0:16], t[:, :, 16:32], sn[:, :, 0:16], ALU.mult)
                        link(g.tensor_tensor(b[:, :, 16:32], t[:, :, 0:16], sn[:, :, 16:32], ALU.mult))
                        g.tensor_tensor(t[:, :, 0:32], a, b, ALU.add).then_inc(rope_done, 1)

                for h in range(SSD_HEADS):
                    ssd_product(h)
                    if h % 4 == 3:
                        rotate(h // 4)

                pool.wait_ge(mix_ready, MIXES * l + 2)
                g.dma_start(p_raw[:, :, :], pT[bass.ds(l, 1)].rearrange("a p k n -> p (a k) n")).then_inc(p_in, 16)

                residual(1)
                g.dma_start(col_in[:, :], cols_in[bass.ds(l, 1)].rearrange("a p n -> p (a n)")
                            ).then_inc(col_in_in, 16)

                def ff_pair(pair, b, again=True):
                    pool.wait_ge(silu_done, FF_TILES * l + pair + 1)
                    pool.wait_ge(conv_done, 2 * FF_TILES * l + 2 * pair + 2)
                    if again:
                        pool.wait_ge(ff_ready, FF_TILES * l + pair - 1)
                    g.tensor_tensor(prod[b][:, :], gs[b][:, :], cv[2 * b + 1][:, :], ALU.mult).then_inc(prod_done, 1)

                def ff_lo(pair, b, kt):
                    pool.wait_ge(ffhi_done, FF_TILES * l + pair + 1)
                    g.tensor_tensor(ffT[:, kt, SEQ:2 * SEQ], prod[b][:, :],
                                    ffT[:, kt, 0:SEQ].bitcast(F32), ALU.subtract).then_inc(ff_ready, 1)

                for first, tiles in ((0, FF1), (FF1, FF2)):
                    ff_pair(first, 0, first > 0)
                    ff_pair(first + 1, 1, first > 0)
                    with pool.Fori(0, tiles // 2 - 1) as u:
                        for b in range(2):
                            pool.wait_ge(ffhi_done, FF_TILES * l + first + 2 * u + b + 1)
                            g.tensor_tensor(ffT[:, bass.ds(2 * u + b, 1), SEQ:2 * SEQ].rearrange("p a n -> p (a n)"),
                                            prod[b][:, :],
                                            ffT[:, bass.ds(2 * u + b, 1), 0:SEQ].rearrange("p a n -> p (a n)")
                                            .bitcast(F32), ALU.subtract).then_inc(ff_ready, 1)
                            ff_pair(first + 2 * u + 2 + b, b)
                    ff_lo(first + tiles - 2, 0, tiles - 2)
                    ff_lo(first + tiles - 1, 1, tiles - 1)
                pool.sem_inc(g_chain, G_CHAIN - count[0])

            pool.wait_ge(ff_ready, FF_TILES * DEPTH)
            g.dma_start(gb_last[:, :, :], gb[2 * DEPTH:2 * DEPTH + 1, :, :].to_broadcast([P, 2, D_MODEL])
                        ).then_inc(gbl_in, 16)
            pool.wait_ge(gbl_in, 16)
            for half in range(HALVES):
                pool.wait_ge(fin_norm, half + 1)
                t = acc[:, half, 0:CHUNK]
                g.tensor_tensor(t, t, gb_last[:, 0, 0:CHUNK], ALU.mult).then_inc(g_chain, 1)
                pool.wait_ge(g_chain, G_CHAIN * DEPTH + half + 1)
                g.tensor_tensor(t, t, gb_last[:, 1, 0:CHUNK], ALU.add).then_inc(ln_res, 1)

        @block.scalar
        def _(act):
            s = nc.scalar

            act.wait_ge(col_in_set, 1)
            s.activation(bn[:, 0, 0:1], col_in[:, 0:1], ACT.Identity)
            act.wait_ge(raw_in[0], 16)
            s.activation(split[0][:, 0, :], raw[0][:, :], ACT.Copy).then_inc(hi_done, 1)

            with act.Fori(0, DEPTH) as l:

                def hi(i, u=None, step=0):
                    more, more_raw = (0, 0) if u is None else (step * u, step // RAW * u)
                    act.wait_ge(raw_in[i % RAW], 16 * (UNITS // RAW * l + more_raw + i // RAW + 1))
                    act.wait_ge(unit_used, UNITS * l + more + i + 1)
                    s.activation(split[i % RING][:, 0, :], raw[i % RAW][:, :], ACT.Copy).then_inc(hi_done, 1)

                def affine(n, unit):
                    c = col_in if n == 0 else col[:, C_L1G:C_L1G + 2 * KT]
                    for kt in range(KT):
                        act.wait_ge(ln_mm, 2 * KT * l + KT * n + kt + 1)
                        if kt >= 2:
                            act.wait_ge(hT_ready, 2 * KT * l + KT * n + kt - 1)
                        s.activation(lnf[kt % 2][:, :], xq[kt % 4][:, 0:SEQ], ACT.Identity, scale=c[:, kt:kt + 1],
                                     bias=c[:, KT + kt:KT + kt + 1]).then_inc(ln_aff, 1)
                        if kt % 4 == 3:
                            hi(unit + kt // 4)

                affine(0, U_V + 1)
                for i in range(U_V + 2, U_XBC):
                    if i == U_V + 7:
                        act.wait_ge(ang_done, l + 1)
                        s.activation(sin[:, :, 0:16], angle[:, 0, :].rearrange("p (h f) -> p h f", f=16), ACT.Sin,
                                     scale=-1.0)
                        s.activation(sin[:, :, 16:32], angle[:, 0, :].rearrange("p (h f) -> p h f", f=16), ACT.Sin)
                        for part in range(2):
                            last = s.activation(cos[:, :, 16 * part:16 * part + 16],
                                                angle[:, 1, :].rearrange("p (h f) -> p h f", f=16), ACT.Sin)
                        last.then_inc(trig_done, 1)
                    if i == U_V + 5:
                        act.wait_ge(par_in, 48 * l + 48)
                        s.activation(wdt_s[:, :, 0:16], wdt_raw[:, :, :], ACT.Copy).then_inc(wdt_hi, 1)
                    hi(i + AHEAD)
                s.activation(row[:, 16:32], row[:, 16:32], ACT.Exp).then_inc(a_exp, 1)
                act.wait_ge(dt_pre, l + 1)
                s.activation(dtx[:, 2, :], dtx[:, 1, :], ACT.Exp, scale=-1.0).then_inc(dt_exp, 1)

                for j in range(XBC_TILES):
                    hi(U_XBC + j + AHEAD)
                    act.wait_ge(xconv_done, XBC_TILES * l + j + 1)
                    dst = bcT[:, j, :] if j < 4 else xbT[:, j - 4, :]
                    s.activation(dst, conv[j % 2][:, :], ACT.Silu).then_inc(xsilu_done, 1)
                for j in range(Z_TILES):
                    hi(U_Z + j + AHEAD)
                    act.wait_ge(gemm_evac, BANKS + GROUPS * l + G_Z + j + 1)
                    s.activation(zs[:, j, :], zs[:, j, :], ACT.Silu).then_inc(zsilu_done, 1)

                def y_square(j):
                    act.wait_ge(yg_done, X_TILES * l + j + 1)
                    if j >= 2:
                        act.wait_ge(yrms_mm, X_TILES * l + j - 1)
                    s.activation(sq[j % 2][:, :], zs[:, j, :], ACT.Square).then_inc(ysq_done, 1)

                def mix_hi(kt, src, tiles=4):
                    s.activation(hT[:, kt:kt + tiles, 0:SEQ], src, ACT.Copy).then_inc(mixhi_done, 1)

                def qkT_evac(c, b):
                    act.wait_ge(qkT_mm, 8 * l + 2 * c + b + 1)
                    dst, h0 = (kT if c % 2 else qT), 4 * (c // 2) + 2 * b
                    s.activation(dst[:, h0:h0 + 2, :], xq[3][:, :].rearrange("p (h t) -> p h t", h=2), ACT.Copy
                                 ).then_inc(qkT_ready, 1)

                for h in range(SSD_HEADS):
                    act.wait_ge(seg_done, SSD_HEADS * l + h + 1)
                    s.activation(seg[h % 2][:, :], seg[h % 2][:, :], ACT.Exp).then_inc(segexp_done, 1)
                    if h >= 3 and h % 2:
                        y_square(h // 2 - 1)
                    if h == 10:
                        act.wait_ge(ln_res, 1 + 4 * CHUNKS * l + 2 * CHUNKS)
                    if h >= 6 and h % 4 >= 2:
                        qkT_evac((h - 6) // 4, h % 4 - 2)
                    if h == SSD_HEADS - 1:
                        act.wait_ge(unit_used, RING + UNITS * l + U_WS - 1)
                        act.wait_ge(yn_done, X_TILES * l + 4)
                        mix_hi(8, zs[:, 0:4, :])
                    hi(U_QK + h + AHEAD)

                y_square(X_TILES - 1)
                act.wait_ge(unit_used, RING + UNITS * l + U_WS)
                act.wait_ge(qkT_mm, 8 * l + 4)
                act.wait_ge(gemm_evac, BANKS + GROUPS * l + G_QK + 6)
                for half in range(HALVES):
                    s.activation(qk_tok[1][:, half, :], gp[(G_QK + 6 + half) % BANKS][:, :], ACT.Copy
                                 ).then_inc(gemm_evac, 1)

                def head_exp(h):
                    act.wait_ge(max_done, HEADS * l + h + 1)
                    t, st = sco[h % 2], stat[:, h % 2, :]
                    s.activation(t[:, 0:128], t[:, 0:128], ACT.Exp, bias=st[:, 0:1], accum_out=st[:, 2:3])
                    s.activation(t[:, 128:384], t[:, 128:384], ACT.Exp, bias=st[:, 1:2], accum_out=st[:, 3:4]
                                 ).then_inc(exp_done, 1)

                def head_prT(h):
                    act.wait_ge(prT_mm, HEADS * l + h + 1)
                    if h >= 2:
                        act.wait_ge(o_mm, HEADS * l + h - 1)
                    s.activation(prT[h % 2][:, :], xq[1][:, 0:384], ACT.Copy).then_inc(prT_ready, 1)

                def head_out(h):
                    act.wait_ge(o_mm, HEADS * l + h + 1)
                    if h >= 2:
                        act.wait_ge(orms_mm, HEADS * l + h - 1)
                    s.activation(oT[:, h, :], xq[2][:, 0:SEQ], ACT.Copy)
                    s.activation(sq[h % 2][:, :], xq[2][:, 0:SEQ], ACT.Square).then_inc(osq_done, 1)

                for h in range(HEADS):
                    if h >= 2:
                        head_out(h - 2)
                    if h >= 1:
                        head_prT(h - 1)
                    if h == 1:
                        act.wait_ge(yn_done, X_TILES * l + 8)
                        mix_hi(12, zs[:, 4:8, :])
                    head_exp(h)
                    if h in (1, 2):
                        qkT_evac(3, h - 1)
                    if h == 5:
                        act.wait_ge(p_in, 16 * l + 16)
                        s.activation(p_s[:, :, 0:SEQ], p_raw[:, :, :], ACT.Copy).then_inc(p_hi, 1)
                    hi(U_WS + h + AHEAD)

                def emb_evac(c):
                    unit, g = (U_PA + c, G_PA + 2 * c) if c < 2 else (U_PB + c - 2, G_PB + 2 * c - 4)
                    act.wait_ge(unit_used, RING + UNITS * l + unit + 1)
                    act.wait_ge(gemm_evac, BANKS + GROUPS * l + g)
                    for half in range(HALVES):
                        s.activation(emb[:, half, c * CHUNK:(c + 1) * CHUNK], gp[(g + half) % BANKS][:, :], ACT.Copy
                                     ).then_inc(gemm_evac, 1)

                head_out(HEADS - 2)
                head_prT(HEADS - 1)
                hi(U_PA + AHEAD)
                head_out(HEADS - 1)
                emb_evac(0)
                emb_evac(1)
                for kt in range(0, HEADS, 2):
                    act.wait_ge(on_done, HEADS * l + kt + 2)
                    mix_hi(kt, oT[:, kt:kt + 2, :], 2)
                hi(U_PA + 1 + AHEAD)
                for i in range(U_WA, U_PB - 1):
                    hi(i + AHEAD)
                hi(U_PB - 1 + AHEAD)
                emb_evac(2)
                emb_evac(3)
                affine(1, U_PB + AHEAD)
                for i in range(U_PB + 4, U_UP1):
                    c, r = divmod(i - U_GATE, 4)
                    hi(i + AHEAD)
                    if r == 3:
                        act.wait_ge(unit_used, RING + UNITS * l + i + 1)
                        for half in range(HALVES):
                            if c:
                                act.wait_ge(gate_read, 2 * CHUNKS * l + 2 * c - 1 + half)
                            s.activation(sig[half][:, :], gp[(G_GATE + 2 * c + half) % BANKS][:, :], ACT.Sigmoid
                                         ).then_inc(gemm_evac, 1)

                def silu(pair, b):
                    act.wait_ge(conv_done, 2 * FF_TILES * l + 2 * pair + 1)
                    act.wait_ge(prod_done, FF_TILES * l + pair + 1)
                    s.activation(gs[b][:, :], cv[2 * b][:, :], ACT.Silu).then_inc(silu_done, 1)

                for first, tiles, u0, d0 in ((0, FF1, U_UP1, U_DN1), (FF1, FF2, U_UP2, U_DN2)):
                    hi(u0 + AHEAD)
                    silu(first, 0)
                    hi(u0 + 1 + AHEAD)
                    with act.Fori(0, tiles // 2 - 1) as u:
                        for b in range(2):
                            i = u0 + 2 + 2 * b
                            act.wait_ge(prod_done, FF_TILES * l + 2 * u + (first + b + 3))
                            s.activation(ffT[:, bass.ds(2 * u + b, 1), 0:SEQ].rearrange("p a n -> p (a n)"),
                                         prod[b][:, :], ACT.Copy).then_inc(ffhi_done, 1)
                            hi(i + AHEAD, u, 4)
                            silu(2 * u + (first + b + 1), (b + 1) % 2)
                            hi(i + 1 + AHEAD, u, 4)
                    last = tiles - 2
                    act.wait_ge(prod_done, FF_TILES * l + first + last + 3)
                    s.activation(ffT[:, last, 0:SEQ], prod[0][:, :], ACT.Copy).then_inc(ffhi_done, 1)
                    hi(u0 + 2 * last + 2 + AHEAD)
                    silu(first + last + 1, 1)
                    hi(u0 + 2 * last + 3 + AHEAD)
                    act.wait_ge(prod_done, FF_TILES * l + first + last + 4)
                    s.activation(ffT[:, last + 1, 0:SEQ], prod[1][:, :], ACT.Copy).then_inc(ffhi_done, 1)
                    if first == 0:
                        with act.Fori(0, 2) as u:
                            for r in range(12):
                                hi(d0 + r + AHEAD, u, 12)
                        act.wait_ge(unit_used, RING + UNITS * l + U_UP2)
                    else:
                        for i in range(d0, UNITS - AHEAD + 1):
                            hi(i + AHEAD)

                act.wait_ge(col_in_in, 16 * l + 16)

            act.wait_ge(factors_ready, 1)
            for half in range(HALVES):
                t = acc[:, half, 0:CHUNK]
                s.activation(t, t, ACT.Identity, scale=ln[:, half, 2:3], bias=ln[:, half, 3:4]).then_inc(fin_norm, 1)

        @block.vector
        def _(dve):
            v = nc.vector

            dve.sem_inc(gemm_evac, BANKS)
            for t in xpad:
                v.memset(t[:, 0:3], 0.0)
            v.memset(ln[:, :, 2], 1.0)
            v.memset(ln[:, :, 3], 0.0)
            v.memset(col_in[:, KT:2 * KT], 0.0)
            v.memset(col_in[:, 0:KT], 1.0).then_inc(col_in_set, 1)

            start = [0]

            def first(ins):
                start[0] += 1
                ins.then_inc(v_chain, 1)
                dve.wait_ge(v_chain, start[0])

            dve.wait_ge(pos_in, 16)
            first(v.tensor_copy(stat[:, 0, 6:8], posi[:, :]))
            dve.wait_ge(start_in, 16)
            v.memset(acsT[:, :].bitcast(I32), 0)
            first(v.memset(pick[:, :].bitcast(I32), 0))
            for p0 in (0, 32):
                v.tensor_copy(pick[p0:p0 + 16, :], ident[p0:p0 + 16, p0:p0 + 16])

            dve.wait_ge(hi_done, 1)
            v.tensor_tensor(split[0][:, 1, :], raw[0][:, :], split[0][:, 0, :].bitcast(F32), ALU.subtract
                            ).then_inc(lo_done, 1)

            with dve.Fori(0, DEPTH) as l:
                count = [start[0]]

                def link(ins):
                    count[0] += 1
                    ins.then_inc(v_chain, 1)
                    dve.wait_ge(v_chain, V_CHAIN * l + count[0])

                def lo(i, u=None, step=0):
                    more = 0 if u is None else step * u
                    dve.wait_ge(hi_done, UNITS * l + more + i + 1)
                    v.tensor_tensor(split[i % RING][:, 1, :], raw[i % RAW][:, :],
                                    split[i % RING][:, 0, :].bitcast(F32), ALU.subtract).then_inc(lo_done, 1)

                def group(g, i, more=0):
                    dve.wait_ge(unit_used, UNITS * l + more + (RING + i + 1))
                    return gp[g % BANKS]

                def sum_parts(g, i, dst, more=0):
                    bank = group(g, i, more)
                    v.tensor_reduce(dst, bank[:, :].rearrange("p (a t) -> p t a", a=2), AX_X, ALU.add
                                    ).then_inc(gemm_evac, 1)

                def normalise(c):
                    for half in range(HALVES):
                        t = acc[:, half, c * CHUNK:(c + 1) * CHUNK]
                        last = v.tensor_scalar(t, t, ln[:, half, 2:3], ln[:, half, 3:4], ALU.mult, ALU.add)
                    last.then_inc(ln_norm, 1)

                def rope_angles():
                    for half in range(HALVES):
                        last = v.tensor_scalar(ang[:, 2, half * 16:half * 16 + 16], cst[:, K_FREQ:K_FREQ + 16],
                                               stat[:, 0, 6 + half:7 + half], None, ALU.mult)
                    link(last)
                    link(v.tensor_scalar(ang[:, 3, :], ang[:, 2, :], float(1 / (2 * np.pi)), None, ALU.mult))
                    link(v.tensor_scalar(ang[:, 3, :], ang[:, 3, :], ROUND, None, ALU.add))
                    link(v.tensor_scalar(ang[:, 3, :], ang[:, 3, :], ROUND, None, ALU.subtract))
                    for part in TWO_PI_PARTS:
                        link(v.scalar_tensor_tensor(ang[:, 2, :], ang[:, 3, :], -part, ang[:, 2, :], ALU.mult, ALU.add))
                    PI = 3.1415925
                    link(v.tensor_scalar(angle[:, 0, :], ang[:, 2, :], PI, -PI, ALU.min, ALU.max))
                    link(v.tensor_scalar(ang[:, 2, :], ang[:, 2, :], float(np.pi / 2), None, ALU.add))
                    link(v.tensor_scalar(ang[:, 4, :], ang[:, 2, :], float(np.pi), -float(2 * np.pi), ALU.is_gt, ALU.mult))
                    link(v.tensor_tensor(ang[:, 2, :], ang[:, 2, :], ang[:, 4, :], ALU.add))
                    v.tensor_scalar(angle[:, 1, :], ang[:, 2, :], PI, -PI, ALU.min, ALU.max).then_inc(ang_done, 1)

                def split_hT(n, unit):
                    for kt in range(KT):
                        dve.wait_ge(ln_aff, 2 * KT * l + KT * n + kt + 1)
                        link(v.tensor_copy(hT[:, kt, 0:SEQ], lnf[kt % 2][:, :]))
                        v.tensor_tensor(hT[:, kt, SEQ:2 * SEQ], lnf[kt % 2][:, :], hT[:, kt, 0:SEQ].bitcast(F32),
                                        ALU.subtract).then_inc(hT_ready, 1)
                        c, r = divmod(kt, 4)
                        if r == 0 and c + 1 < CHUNKS:
                            if n == 0:
                                dve.wait_ge(x_in[c + 1], 16)
                            normalise(c + 1)
                        if r == 3:
                            lo(unit + c)

                dve.wait_ge(x_in[0], 16)
                normalise(0)
                split_hT(0, U_V + 1)
                for c in range(2):
                    for r in range(4):
                        if r == 0 and c:
                            for half in range(HALVES):
                                v.tensor_copy(v_tok[:, half, 0:CHUNK], group(half, U_V + 3)[:, :]).then_inc(gemm_evac, 1)
                        if c == 1 and r == 1:
                            rope_angles()
                        if c == 1 and r == 2:
                            dve.wait_ge(wdt_hi, l + 1)
                            v.tensor_tensor(wdt_s[:, :, 16:32], wdt_raw[:, :, :], wdt_s[:, :, 0:16].bitcast(F32),
                                            ALU.subtract).then_inc(wdt_ready, 1)
                        if 4 * c + r >= 2:
                            lo(U_V + 4 * c + r + AHEAD)
                for half in range(HALVES):
                    v.tensor_copy(v_tok[:, half, CHUNK:2 * CHUNK], group(2 + half, U_V + 7)[:, :]).then_inc(gemm_evac, 1)

                dve.wait_ge(dt_mm, l + 1)
                link(v.tensor_reduce(dtx[:, 0, :].rearrange("p (h n) -> p h n", n=16),
                                     xq[0][:, 0:64].rearrange("p (h a n) -> p h n a", h=2, a=2), AX_X, ALU.add))
                for half in range(HALVES):
                    t = dtx[:, 0, 16 * half:16 * half + 16]
                    last = v.tensor_tensor(t, t, row[:, 0:16], ALU.add)
                link(last)
                v.scalar_tensor_tensor(dtx[:, 1, :], dtx[:, 0, :], -1.0, dtx[:, 0, :], ALU.mult, ALU.max).then_inc(dt_pre, 1)
                dve.wait_ge(dt_exp, l + 1)
                link(v.tensor_scalar(dtx[:, 3, :], dtx[:, 2, :], 2.0, None, ALU.add))
                link(v.reciprocal(dtx[:, 4, :], dtx[:, 3, :]))
                link(v.tensor_tensor(dtx[:, 5, :], dtx[:, 4, :], dtx[:, 2, :], ALU.mult))
                link(v.tensor_tensor(dtx[:, 6, :], dtx[:, 5, :], dtx[:, 5, :], ALU.mult))
                link(v.tensor_scalar(dtx[:, 7, :], dtx[:, 6, :], 1.0 / 17, None, ALU.mult))
                for n in (15, 13, 11, 9, 7, 5, 3):
                    link(v.scalar_tensor_tensor(dtx[:, 7, :], dtx[:, 7, :], 1.0 / n, dtx[:, 6, :], ALU.add, ALU.mult))
                v.scalar_tensor_tensor(dtx[:, 4, :], dtx[:, 7, :], 1.0, dtx[:, 5, :], ALU.add, ALU.mult)
                link(v.tensor_scalar(dtx[:, 3, :], dtx[:, 0, :], 0.0, None, ALU.max))
                link(v.scalar_tensor_tensor(dtx[:, 10, :], dtx[:, 4, :], 2.0, dtx[:, 3, :], ALU.mult, ALU.add))
                dve.wait_ge(a_exp, l + 1)
                for half in range(HALVES):
                    v.scalar_tensor_tensor(dtx[:, 11, 16 * half:16 * half + 16], dtx[:, 10, 16 * half:16 * half + 16],
                                           -1.0, row[:, 16:32], ALU.mult, ALU.mult).then_inc(da_ready, 1)

                def taps(xp, o, w, n, b):
                    link(v.tensor_scalar(o[:, :], xp[:, 3:3 + SEQ], w(n - 1), b, ALU.mult, ALU.add))
                    for k in range(n - 1):
                        last = v.scalar_tensor_tensor(o[:, :], xp[:, 4 - n + k:4 - n + k + SEQ], w(k), o[:, :],
                                                      ALU.mult, ALU.add)
                        if k < n - 2:
                            link(last)
                    return last

                for j in range(XBC_TILES):
                    xp, o = xpad[j % 2], conv[j % 2]
                    sum_parts(G_XBC + j, U_XBC + j, xp[:, 3:3 + SEQ])
                    dve.wait_ge(gemm_evac, BANKS + GROUPS * l + G_XBC + j + 1)
                    if j >= 2:
                        dve.wait_ge(xsilu_done, XBC_TILES * l + j - 1)
                    taps(xp, o, lambda k: col[:, C_XW + 4 * j + k:C_XW + 4 * j + k + 1], 4,
                         col[:, C_XB + j:C_XB + j + 1]).then_inc(xconv_done, 1)
                    if j == 3:
                        dve.wait_ge(acs_mm, l + 1)
                        v.tensor_copy(acs[:, :, :], xq[1][:, 0:32].rearrange("p (h n) -> p h n", h=2)
                                      ).then_inc(acs_ready, 1)
                    if j == 6:
                        dve.wait_ge(acsT_mm, l + 1)
                        link(v.tensor_copy(acsT[0:16, :], xq[2][0:16, 0:SEQ]))
                        v.tensor_tensor(acsT[32:48, :], xq[2][0:16, 0:SEQ], acsT[0:16, :].bitcast(F32), ALU.subtract
                                        ).then_inc(acsT_ready, 1)
                    lo(U_XBC + j + AHEAD)

                for j in range(Z_TILES):
                    sum_parts(G_Z + j, U_Z + j, zs[:, j, :])
                    if j in (1, 2):
                        dve.wait_ge(cb_mm, SSD_GROUPS * l + j)
                        v.tensor_copy(cb[:, j - 1, :], xq[j][:, 0:384]).then_inc(cb_ready, 1)
                    if 3 <= j < 7:
                        half, q = (j - 3) // 2, (j - 3) % 2
                        dve.wait_ge(xt_mm, 4 * l + j - 2)
                        bank = xq[3 if j % 2 else 0]
                        v.tensor_tensor(xdt[:, half, CHUNK * q:CHUNK * (q + 1)].rearrange("p (h d) -> p h d", d=SSD_HD),
                                        bank[:, :].rearrange("p (h d) -> p h d", d=SSD_HD),
                                        dtx[:, 10, 16 * half + 8 * q:16 * half + 8 * q + 8].unsqueeze(2)
                                        .to_broadcast([P, 8, SSD_HD]), ALU.mult).then_inc(xdt_ready, 1)
                    lo(U_Z + j + AHEAD)

                def qk_out(c):
                    for half in range(HALVES):
                        if c >= 2:
                            dve.wait_ge(qkT_mm, 8 * l + 2 * c - 2)
                        v.tensor_copy(qk_tok[c % 2][:, half, :], group(G_QK + 2 * c + half, U_QK + 4 * c + 3)[:, :]
                                      ).then_inc(gemm_evac, 1)

                def y_gate(j):
                    dve.wait_ge(y_mm, SSD_HEADS * l + 2 * j + 2)
                    v.scalar_tensor_tensor(tmp, xbT[:, j, :], col[:, C_D + j:C_D + j + 1], xq[1][:, 0:SEQ],
                                           ALU.mult, ALU.add).then_inc(y_read, 1)
                    dve.wait_ge(y_read, X_TILES * l + j + 1)
                    dve.wait_ge(zsilu_done, Z_TILES * l + j + 1)
                    v.tensor_tensor(zs[:, j, :], zs[:, j, :], tmp, ALU.mult).then_inc(yg_done, 1)

                def inverse_root():
                    link(v.tensor_scalar(ln[:, :, 5].bitcast(I32), ln[:, :, 4].bitcast(I32), 1, None,
                                         ALU.arith_shift_right))
                    link(v.tensor_scalar(ln[:, :, 2].bitcast(I32), ln[:, :, 5].bitcast(I32), -1.0, float(0x5f3759df),
                                         ALU.mult, ALU.add))
                    for _ in range(3):
                        link(v.scalar_tensor_tensor(ln[:, :, 5], ln[:, :, 2], -0.5, ln[:, :, 4], ALU.mult, ALU.mult))
                        link(v.tensor_tensor(ln[:, :, 5], ln[:, :, 5], ln[:, :, 2], ALU.mult))
                        link(v.scalar_tensor_tensor(ln[:, :, 2], ln[:, :, 5], 1.5, ln[:, :, 2], ALU.add, ALU.mult))

                def mean_square(bank, width):
                    return v.tensor_scalar(ln[:, :, 4], bank[:, SEQ:SEQ + HALVES], 1.0 / width, RMS_EPS,
                                           ALU.mult, ALU.add)

                def root_diagonal():
                    inverse_root()
                    for half in range(HALVES):
                        last = v.tensor_scalar(rms_s[:, P * half:P * (half + 1)], ident, ln[:, half, 2:3], None, ALU.mult)
                    last.then_inc(root_done, 1)

                def y_root(g):
                    dve.wait_ge(yrms_mm, X_TILES * l + 4 * g + 4)
                    mean_square(xq[2], 512).then_inc(yrms_read, 1)
                    dve.wait_ge(yrms_read, SSD_GROUPS * l + g + 1)
                    root_diagonal()

                def y_norm(g):
                    dve.wait_ge(spread_mm, 3 * l + g + 1)
                    for j in range(4 * g, 4 * g + 4):
                        v.scalar_tensor_tensor(zs[:, j, :], zs[:, j, :], col[:, C_SN + j:C_SN + j + 1],
                                               xq[2][:, 0:SEQ], ALU.mult, ALU.mult).then_inc(yn_done, 1)

                def mix_lo(kt, src, m, tiles=4):
                    dve.wait_ge(mixhi_done, MIXES * l + m + 1)
                    v.tensor_tensor(hT[:, kt:kt + tiles, SEQ:2 * SEQ], src, hT[:, kt:kt + tiles, 0:SEQ]
                                    .bitcast(F32), ALU.subtract).then_inc(mix_ready, 1)

                for h in range(SSD_HEADS):
                    if h and h % 4 == 0:
                        qk_out(h // 4 - 1)
                    dve.wait_ge(row_mm, SSD_HEADS * l + h + 1)
                    if h >= 2:
                        dve.wait_ge(m_done, SSD_HEADS * l + h - 1)
                    v.scalar_tensor_tensor(seg[h % 2][:, 0:256], xq[0][:, 0:256], acs[:, 0, h:h + 1], smask[:, 0:256],
                                           ALU.subtract, ALU.add)
                    v.scalar_tensor_tensor(seg[h % 2][:, 256:384], xq[0][:, 128:256], acs[:, 1, h:h + 1],
                                           smask[:, 0:128], ALU.subtract, ALU.add).then_inc(seg_done, 1)
                    if h >= 3 and h % 2:
                        y_gate(h // 2 - 1)
                    if h == 11:
                        y_root(0)
                    if h == 12:
                        y_norm(0)
                    if h == SSD_HEADS - 1:
                        mix_lo(8, zs[:, 0:4, :], 0)
                        y_gate(X_TILES - 1)
                    lo(U_QK + h + AHEAD)


                def head_scores(h):
                    t, st = sco[h % 2], stat[:, h % 2, :]
                    dve.wait_ge(sc_mm, HEADS * l + h + 1)
                    if h == 0:
                        dve.wait_ge(m_done, SSD_HEADS * l + SSD_HEADS)
                    if h >= 2:
                        dve.wait_ge(prT_mm, HEADS * l + h - 1)
                    v.scalar_tensor_tensor(t[:, :], xq[0][:, 0:384], SCALE, amask, ALU.mult, ALU.add
                                           ).then_inc(sc_read, 1)
                    dve.wait_ge(sc_read, HEADS * l + h + 1)
                    v.tensor_reduce(st[:, 0:1], t[:, 0:128], AX_X, ALU.max, negate=True)
                    v.tensor_reduce(st[:, 1:2], t[:, 128:384], AX_X, ALU.max, negate=True).then_inc(max_done, 1)

                def head_probs(h):
                    t, st = sco[h % 2], stat[:, h % 2, :]
                    dve.wait_ge(exp_done, HEADS * l + h + 1)
                    link(v.reciprocal(st[:, 4:6], st[:, 2:4]))
                    v.tensor_scalar(t[:, 0:128], t[:, 0:128], st[:, 4:5], None, ALU.mult)
                    v.tensor_scalar(t[:, 128:384], t[:, 128:384], st[:, 5:6], None, ALU.mult).then_inc(prob_done, 1)

                def out_rows(g, i, c, half, keep_scale, more=0, dc=None):
                    bank = group(g, i, more)
                    t = (acc[:, half, c * CHUNK:(c + 1) * CHUNK] if dc is None
                         else acc[:, half, bass.ds(dc + c * CHUNK, CHUNK)])
                    if keep_scale:
                        v.scalar_tensor_tensor(t, t, ALPHA, bank[:, :], ALU.mult, ALU.add).then_inc(gemm_evac, 1)
                    else:
                        v.tensor_tensor(t, t, bank[:, :], ALU.add).then_inc(gemm_evac, 1)

                for h in range(HEADS):
                    if h == 1:
                        y_norm(1)
                    head_scores(h)
                    if h == 1:
                        mix_lo(12, zs[:, 4:8, :], 1)
                    head_probs(h)
                    if h == 0:
                        y_root(1)
                    if h == 3:
                        dve.wait_ge(ln_res, 1 + 4 * CHUNKS * l + 2 * CHUNKS)
                    if h in (3, 4, 6):
                        c = {3: 0, 4: 1, 6: 2}[h]
                        for half in range(HALVES):
                            out_rows(G_WS + 2 * c + half, U_WS + h - 1, c, half, True)
                    if h == 6:
                        dve.wait_ge(p_hi, l + 1)
                        v.tensor_tensor(p_s[:, :, SEQ:2 * SEQ], p_raw[:, :, :], p_s[:, :, 0:SEQ].bitcast(F32),
                                        ALU.subtract).then_inc(p_ready, 1)
                    lo(U_WS + h + AHEAD)
                for half in range(HALVES):
                    out_rows(G_WS + 6 + half, U_WS + 7, 3, half, True)
                lo(U_PA + AHEAD)

                dve.wait_ge(orms_mm, HEADS * l + HEADS)
                mean_square(xq[3], ATTN_WIDTH).then_inc(orms_read, 1)
                dve.wait_ge(orms_read, l + 1)
                root_diagonal()
                dve.wait_ge(spread_mm, 3 * l + 3)
                for h in range(HEADS):
                    v.scalar_tensor_tensor(oT[:, h, :], oT[:, h, :], col[:, C_AN + h:C_AN + h + 1],
                                           xq[3][:, 0:SEQ], ALU.mult, ALU.mult).then_inc(on_done, 1)
                    if h >= 3 and h % 2:
                        mix_lo(h - 3, oT[:, h - 3:h - 1, :], 2 + h // 2 - 1, 2)
                mix_lo(HEADS - 2, oT[:, HEADS - 2:HEADS, :], MIXES - 1, 2)
                lo(U_PA + 1 + AHEAD)

                def rows_and_stats(g, i, c, early=None):
                    if early:
                        dve.wait_ge(half_done, 2 * l + early)
                        t = acc[:, 0, c * CHUNK:(c + 1) * CHUNK]
                        v.tensor_tensor(t, t, gp[g % BANKS][:, :], ALU.add).then_inc(gemm_evac, 1)
                        dve.wait_ge(gemm_evac, BANKS + GROUPS * l + g + 1)
                        v.bn_stats(bn[:, 0, 6 * c:6 * c + 6], t)
                        out_rows(g + 1, i, c, 1, False)
                        dve.wait_ge(gemm_evac, BANKS + GROUPS * l + g + 2)
                        return v.bn_stats(bn[:, 1, 6 * c:6 * c + 6], acc[:, 1, c * CHUNK:(c + 1) * CHUNK])
                    for half in range(HALVES):
                        out_rows(g + half, i, c, half, False)
                    for half in range(HALVES):
                        dve.wait_ge(gemm_evac, BANKS + GROUPS * l + g + half + 1)
                        last = v.bn_stats(bn[:, half, 6 * c:6 * c + 6], acc[:, half, c * CHUNK:(c + 1) * CHUNK])
                    return last

                def norm_factors():
                    v.memset(ln[:, :, 5], 0.0)
                    for half in range(HALVES):
                        last = v.bn_aggr(ln[:, half, 0:2], bn[:, half, :])
                    link(last)
                    link(v.tensor_scalar(ln[:, :, 4], ln[:, :, 1], LN_EPS, None, ALU.add))
                    inverse_root()
                    link(v.scalar_tensor_tensor(ln[:, :, 3], ln[:, :, 0], -1.0, ln[:, :, 2], ALU.mult, ALU.mult))

                for c in range(CHUNKS):
                    if c == 0:
                        dve.wait_ge(gemm_evac, BANKS + GROUPS * l + G_WA)
                    lo(U_WA + 2 * c + AHEAD)
                    if c:
                        rows_and_stats(G_WA + 2 * c - 2, U_WA + 2 * c - 1, c - 1)
                    lo(U_WA + 2 * c + 1 + AHEAD)
                link(rows_and_stats(G_WA + 6, U_WA + 7, 3, 1))
                norm_factors()
                normalise(0)
                split_hT(1, U_PB + AHEAD)

                def gate_rows(c):
                    for half in range(HALVES):
                        cols_c = slice(c * CHUNK, (c + 1) * CHUNK)
                        dve.wait_ge(gemm_evac, BANKS + GROUPS * l + G_GATE + 2 * c + half + 1)
                        v.tensor_tensor(gated[half][:, :], emb[:, half, cols_c], sig[half][:, :], ALU.mult
                                        ).then_inc(gate_read, 1)
                        dve.wait_ge(gate_read, 2 * CHUNKS * l + 2 * c + half + 1)
                        dve.wait_ge(ln_res, 1 + 4 * CHUNKS * l + 2 * CHUNKS + 2 * c + half + 1)
                        t = acc[:, half, cols_c]
                        last = v.scalar_tensor_tensor(t, t, ALPHA, gated[half][:, :], ALU.mult, ALU.add)
                    if c < CHUNKS - 1:
                        link(last)

                for i in range(U_PB + 4, U_UP1):
                    c, r = divmod(i - U_GATE, 4)
                    lo(i + AHEAD)
                    if c and r == 0:
                        gate_rows(c - 1)
                gate_rows(CHUNKS - 1)

                for first_pair, tiles, u0, d0, gu, gd in ((0, FF1, U_UP1, U_DN1, G_UP1, G_DN1),
                                                          (FF1, FF2, U_UP2, U_DN2, G_UP2, G_DN2)):
                    with dve.Fori(0, tiles // 2) as u:
                        links = [count[0]]

                        def loop_link(ins):
                            links[0] += 1
                            ins.then_inc(v_chain, 1)
                            dve.wait_ge(v_chain, V_CHAIN * l + 8 * u + links[0])

                        for j in range(4):
                            xp, o = xpad[j % 2], cv[j]
                            sum_parts(gu + j, u0 + j, xp[:, 3:3 + SEQ], 4 * u)
                            dve.wait_ge(gemm_evac, GROUPS * l + 4 * u + (BANKS + gu + j + 1))
                            dve.wait_ge(prod_done, FF_TILES * l + 2 * u + (first_pair + j // 2 + 1))
                            tile = 2 * first_pair + j
                            w = [col[:, bass.ds(12 * u + (C_FW + 3 * tile + k), 1)] for k in range(3)]
                            b = col[:, bass.ds(4 * u + (C_FB + tile), 1)]
                            loop_link(v.tensor_scalar(o[:, :], xp[:, 3:3 + SEQ], w[2], b, ALU.mult, ALU.add))
                            loop_link(v.scalar_tensor_tensor(o[:, :], xp[:, 1:1 + SEQ], w[0], o[:, :],
                                                             ALU.mult, ALU.add))
                            v.scalar_tensor_tensor(o[:, :], xp[:, 2:2 + SEQ], w[1], o[:, :], ALU.mult, ALU.add
                                                   ).then_inc(conv_done, 1)
                            lo(u0 + j + AHEAD, u, 4)
                        assert links[0] - count[0] == 8
                    count[0] += 8 * (tiles // 2)
                    if first_pair == 0:
                        with dve.Fori(0, 2) as u:
                            for cc in range(2):
                                for r in range(6):
                                    lo(d0 + 6 * cc + r + AHEAD, u, 12)
                                for half in range(HALVES):
                                    out_rows(gd + 2 * cc + half, d0 + 6 * cc + 5, cc, half, False, 12 * u, 2 * CHUNK * u)
                    else:
                        for c in range(CHUNKS):
                            for r in range(5):
                                if c and r == 1:
                                    rows_and_stats(gd + 2 * c - 2, d0 + 5 * c - 1, c - 1)
                                if d0 + 5 * c + r + AHEAD <= UNITS:
                                    lo(d0 + 5 * c + r + AHEAD)
                link(rows_and_stats(G_DN2 + 6, UNITS - 1, 3, 2))
                norm_factors()
                assert count[0] - start[0] < V_CHAIN, count
                dve.sem_inc(v_chain, V_CHAIN - (count[0] - start[0]))

            dve.sem_inc(factors_ready, 1)
            dve.wait_ge(gbl_in, 16)
            for n in range(2, 2 * CHUNKS):
                c, half = n // 2, n % 2
                t = acc[:, half, c * CHUNK:(c + 1) * CHUNK]
                v.scalar_tensor_tensor(t, t, ln[:, half, 0:1], gb_last[:, 0, c * CHUNK:(c + 1) * CHUNK],
                                       ALU.subtract, ALU.mult).then_inc(v_chain, 1)
                dve.wait_ge(v_chain, start[0] + V_CHAIN * DEPTH + n - 1)
                v.scalar_tensor_tensor(t, t, ln[:, half, 2:3], gb_last[:, 1, c * CHUNK:(c + 1) * CHUNK],
                                       ALU.mult, ALU.add).then_inc(fin_done, 1)

        @block.tensor
        def _(pe):
            t = nc.tensor

            def mm_(out_ap, lhsT, rhs, start, stop):
                return t.matmul(out_ap, lhsT, rhs, start=start, stop=stop, skip_group_check=True)

            pe.sem_inc(unit_used, RING)
            pe.wait_ge(start_in, 16)

            with pe.Fori(0, DEPTH) as l:

                def weights_of(i, u=None, step=0):
                    pe.wait_ge(lo_done, UNITS * l + (0 if u is None else step * u) + i + 1)
                    return split[i % RING]

                def bank_free(g, more=0):
                    pe.wait_ge(gemm_evac, GROUPS * l + more + g + 1)
                    return gp[g % BANKS]

                def last_unit(i, lhs, kts, g):
                    w = weights_of(i)
                    for half in range(HALVES):
                        bank = gp[(g + half) % BANKS]
                        for n, kt in enumerate(kts):
                            w_hi, w_lo = (w[:, part, CHUNK * n:CHUNK * (n + 1)] for part in range(2))
                            a_hi = lhs[:, kt, P * half:P * (half + 1)]
                            a_lo = lhs[:, kt, SEQ + P * half:SEQ + P * (half + 1)]
                            mm_(bank[:, :], a_hi, w_hi, False, False)
                            mm_(bank[:, :], a_hi, w_lo, False, False)
                            ins = mm_(bank[:, :], a_lo, w_hi, False, n == len(kts) - 1)
                        if half == 0:
                            ins.then_inc(half_done, 1)
                    ins.then_inc(unit_used, 1)

                def a_unit(i, lhs, kts, g, first, last, ready=None, u=None, step=0, more=0):
                    w = weights_of(i, u, step)
                    banks = [bank_free(g + half, more) if first else gp[(g + half) % BANKS]
                             for half in range(HALVES)]
                    for n, kt in enumerate(kts):
                        if ready is not None:
                            ready(kt)
                        w_hi, w_lo = (w[:, part, CHUNK * n:CHUNK * (n + 1)] for part in range(2))
                        for half in range(HALVES):
                            a_hi = lhs[:, kt, P * half:P * (half + 1)]
                            a_lo = lhs[:, kt, SEQ + P * half:SEQ + P * (half + 1)]
                            mm_(banks[half][:, :], a_hi, w_hi, first and n == 0, False)
                            mm_(banks[half][:, :], a_hi, w_lo, False, False)
                            ins = mm_(banks[half][:, :], a_lo, w_hi, False, last and n == len(kts) - 1)
                    ins.then_inc(unit_used, 1)

                def b_unit(i, g, u=None, step=0, more=0):
                    w = weights_of(i, u, step)
                    bank = bank_free(g, more)
                    for kt in range(KT):
                        mm_(bank[:, :], w[:, 0, P * kt:P * (kt + 1)], hT[:, kt, :], kt == 0, False)
                        ins = mm_(bank[:, 0:SEQ], w[:, 1, P * kt:P * (kt + 1)], hT[:, kt, 0:SEQ], False, kt == KT - 1)
                    ins.then_inc(unit_used, 1)

                def norm_transpose(n, kt):
                    if kt % 4 == 0:
                        pe.wait_ge(ln_norm, 2 * CHUNKS * l + CHUNKS * n + kt // 4 + 1)
                    if kt >= 4:
                        pe.wait_ge(ln_aff, 2 * KT * l + KT * n + kt - 3)
                    for half in range(HALVES):
                        ins = t.transpose(xq[kt % 4][:, P * half:P * (half + 1)],
                                          acc[:, half, P * kt:P * (kt + 1)], ident)
                    ins.then_inc(ln_mm, 1)

                def new_hT(n):
                    def ready(kt):
                        if 1 <= kt <= KT - 4:
                            norm_transpose(n, kt + 3)
                        pe.wait_ge(hT_ready, 2 * KT * l + KT * n + kt + 1)
                    return ready

                for kt in range(4):
                    norm_transpose(0, kt)
                for c in range(2):
                    for r in range(4):
                        a_unit(U_V + 4 * c + r, hT, range(4 * r, 4 * r + 4), G_V + 2 * c, r == 0, r == 3,
                               new_hT(0) if c == 0 else None)
                pe.wait_ge(wdt_ready, l + 1)
                for half in range(HALVES):
                    for kt in range(KT):
                        mm_(xq[0][:, 32 * half:32 * half + 32], hT[:, kt, P * half:P * (half + 1)], wdt_s[:, kt, :],
                            kt == 0, False)
                        ins = mm_(xq[0][:, 32 * half:32 * half + 16], hT[:, kt, SEQ + P * half:SEQ + P * (half + 1)],
                                  wdt_s[:, kt, 0:16], False, kt == KT - 1)
                ins.then_inc(dt_mm, 1)

                for j in range(XBC_TILES):
                    if j == 2:
                        pe.wait_ge(da_ready, 2 * l + 2)
                        da = [dtx[:, 11, 16 * half:16 * half + 16] for half in range(HALVES)]
                        mm_(xq[1][:, 0:16], tri, da[0], True, True)
                        mm_(xq[1][:, 16:32], ones, da[0], True, False)
                        mm_(xq[1][:, 16:32], tri, da[1], False, True).then_inc(acs_mm, 1)
                    if j == 5:
                        pe.wait_ge(acs_ready, l + 1)
                        for half in range(HALVES):
                            ins = t.transpose(xq[2][0:16, P * half:P * (half + 1)], acs[:, half, :], ident)
                        ins.then_inc(acsT_mm, 1)
                    b_unit(U_XBC + j, G_XBC + j)

                for j in range(Z_TILES):
                    if j in (1, 2):
                        g = j - 1
                        if g == 0:
                            pe.wait_ge(xsilu_done, XBC_TILES * l + XBC_TILES)
                            pe.wait_ge(acsT_ready, l + 1)
                        mm_(xq[j][:, 0:256], bcT[:, g, 0:P], bcT[:, 2 + g, :], True, True)
                        mm_(xq[j][:, 256:384], bcT[:, g, P:SEQ], bcT[:, 2 + g, P:SEQ], True, True).then_inc(cb_mm, 1)
                    if 3 <= j < 7:
                        half, q = (j - 3) // 2, (j - 3) % 2
                        if j >= 5:
                            pe.wait_ge(xdt_ready, 4 * l + j - 4)
                        for n in range(4):
                            ins = t.transpose(xq[3 if j % 2 else 0][:, P * n:P * (n + 1)],
                                              xbT[:, 4 * q + n, P * half:P * (half + 1)], ident)
                        ins.then_inc(xt_mm, 1)
                    b_unit(U_Z + j, G_Z + j)

                def decay_row(h):
                    if h:
                        pe.wait_ge(seg_done, SSD_HEADS * l + h)
                    else:
                        pe.wait_ge(xdt_ready, 4 * l + 4)
                    mm_(xq[0][:, 0:SEQ], pick[:, h:h + 1].to_broadcast([48, P]), acsT[:, :], True, True
                        ).then_inc(row_mm, 1)

                def y_head(h):
                    if h == 0:
                        pe.wait_ge(cb_ready, SSD_GROUPS * l + 2)
                        pe.wait_ge(xdt_ready, 4 * l + 4)
                    elif h % 2 == 0:
                        pe.wait_ge(y_read, X_TILES * l + h // 2)
                    pe.wait_ge(m_done, SSD_HEADS * l + h + 1)
                    p0 = SSD_HD * (h % 2)
                    mm_(xq[1][p0:p0 + SSD_HD, 0:SEQ], xdt[:, 0, SSD_HD * h:SSD_HD * (h + 1)], mm[h % 2][:, 0:256],
                        True, False)
                    mm_(xq[1][p0:p0 + SSD_HD, P:SEQ], xdt[:, 1, SSD_HD * h:SSD_HD * (h + 1)], mm[h % 2][:, 256:384],
                        False, True).then_inc(y_mm, 1)

                def token_sums(bank, squares, start, stop):
                    for half in range(HALVES):
                        one_column = cst[:, K_COL + 1 - half:K_COL + 3 - half]
                        ins = mm_(bank[:, SEQ:SEQ + 2], squares[:, P * half:P * (half + 1)], one_column,
                                  start and half == 0, stop and half == 1)
                    return ins

                def y_sums(j):
                    if j == 4:
                        pe.wait_ge(yn_done, X_TILES * l + 4)
                    pe.wait_ge(ysq_done, X_TILES * l + j + 1)
                    token_sums(xq[2], sq[j % 2], j % 4 == 0, j % 4 == 3).then_inc(yrms_mm, 1)

                def spread(bank, n):
                    pe.wait_ge(root_done, 3 * l + n + 1)
                    mm_(bank[:, 0:SEQ], ones, rms_s[:, :], True, True).then_inc(spread_mm, 1)

                def qk_transposes(c, b):
                    pe.wait_ge(rope_done, 8 * l + 2 * c + 2)
                    if c or b:
                        pe.wait_ge(qkT_ready, 8 * l + 2 * c + b)
                    for n in range(2):
                        for half in range(HALVES):
                            ins = t.transpose(xq[3][:, SEQ * n + P * half:SEQ * n + P * (half + 1)],
                                              qk_tok[c % 2][:, half, HD * (2 * b + n):HD * (2 * b + n + 1)], ident)
                    ins.then_inc(qkT_mm, 1)

                def first_spread(kt):
                    if kt == 2:
                        spread(xq[2], 0)

                for h in range(SSD_HEADS):
                    if h >= 2:
                        y_head(h - 2)
                    decay_row(h)
                    if h in (4, 6, 8, 10):
                        y_sums(h // 2 - 2)
                    if h in (13, 14):
                        y_sums(h - 9)
                    if h >= 6 and h % 4 >= 2:
                        qk_transposes((h - 6) // 4, h % 4 - 2)
                    a_unit(U_QK + h, hT, range(4 * (h % 4), 4 * (h % 4) + 4), G_QK + 2 * (h // 4), h % 4 == 0,
                           h % 4 == 3, first_spread if h == 12 else None)
                y_head(SSD_HEADS - 2)
                y_head(SSD_HEADS - 1)

                def scores(h):
                    if h == 0:
                        pe.wait_ge(seg_done, SSD_HEADS * l + SSD_HEADS)
                    else:
                        pe.wait_ge(sc_read, HEADS * l + h)
                    if h == 0:
                        pe.wait_ge(qkT_ready, 8 * l + 4)
                    elif h == 4:
                        pe.wait_ge(qkT_ready, 8 * l + 8)
                    mm_(xq[0][:, 0:128], qT[:, h, 0:P], kT[:, h, 0:P], True, True)
                    mm_(xq[0][:, 128:384], qT[:, h, P:SEQ], kT[:, h, :], True, True).then_inc(sc_mm, 1)

                def prob_transposes(h):
                    if h:
                        pe.wait_ge(prT_ready, HEADS * l + h)
                    pe.wait_ge(prob_done, HEADS * l + h + 1)
                    for n in range(3):
                        ins = t.transpose(xq[1][:, P * n:P * (n + 1)], sco[h % 2][:, P * n:P * (n + 1)], ident)
                    ins.then_inc(prT_mm, 1)

                def values(h):
                    if h:
                        pe.wait_ge(osq_done, HEADS * l + h)
                    else:
                        pe.wait_ge(yn_done, X_TILES * l + 8)
                    pe.wait_ge(prT_ready, HEADS * l + h + 1)
                    mm_(xq[2][:, 0:SEQ], v_tok[:, 0, HD * h:HD * (h + 1)], prT[h % 2][:, 0:256], True, False)
                    mm_(xq[2][:, P:SEQ], v_tok[:, 1, HD * h:HD * (h + 1)], prT[h % 2][:, 256:384], False, True
                        ).then_inc(o_mm, 1)

                def out_sums(h):
                    if h == 0:
                        pe.wait_ge(qkT_ready, 8 * l + 8)
                    pe.wait_ge(osq_done, HEADS * l + h + 1)
                    token_sums(xq[3], sq[h % 2], h == 0, h == HEADS - 1).then_inc(orms_mm, 1)

                def last_y_sums(kt):
                    if kt == 10:
                        y_sums(X_TILES - 2)
                        y_sums(X_TILES - 1)

                def second_spread(kt):
                    if kt == 9:
                        spread(xq[2], 1)

                for h in range(HEADS):
                    if h >= 2:
                        values(h - 2)
                    if h >= 1:
                        prob_transposes(h - 1)
                    scores(h)
                    if h in (1, 2):
                        qk_transposes(3, h - 1)
                    if h >= 3:
                        out_sums(h - 3)
                    c, part = WS_ORDER[h]
                    if h in (0, 2):
                        pe.wait_ge(mix_ready, MIXES * l + part + 1)
                    a_unit(U_WS + h, hT, range(8 + 4 * part, 12 + 4 * part), G_WS + 2 * c, part == 0, part == 1,
                           last_y_sums if h == 0 else second_spread if h == 1 else None)

                def embed(i, g):
                    a_unit(i, p_s, range(2), g, True, True)

                values(HEADS - 2)
                prob_transposes(HEADS - 1)
                out_sums(HEADS - 3)
                pe.wait_ge(p_ready, l + 1)
                embed(U_PA, G_PA)
                values(HEADS - 1)
                out_sums(HEADS - 2)
                out_sums(HEADS - 1)
                embed(U_PA + 1, G_PA + 2)
                spread(xq[3], 2)
                def pair_ready(kt):
                    if kt % 2 == 0:
                        pe.wait_ge(mix_ready, MIXES * l + 3 + kt // 2)

                for r in range(7):
                    a_unit(U_WA + r, hT, range(4 * (r % 2), 4 * (r % 2) + 4), G_WA + 2 * (r // 2), r % 2 == 0,
                           r % 2 == 1, pair_ready if r < 2 else None)
                last_unit(U_WA + 7, hT, range(4, 8), G_WA + 6)
                for n in range(2):
                    embed(U_PB + n, G_PB + 2 * n)
                for kt in range(4):
                    norm_transpose(1, kt)
                for c in range(CHUNKS):
                    for r in range(4):
                        a_unit(U_GATE + 4 * c + r, hT, range(4 * r, 4 * r + 4), G_GATE + 2 * c, r == 0, r == 3,
                               new_hT(1) if c == 0 else None)

                for first, tiles, u0, d0, gu, gd in ((0, FF1, U_UP1, U_DN1, G_UP1, G_DN1),
                                                     (FF1, FF2, U_UP2, U_DN2, G_UP2, G_DN2)):
                    with pe.Fori(0, tiles // 2) as u:
                        for j in range(4):
                            b_unit(u0 + j, gu + j, u, 4, 4 * u)

                    def down(i, c, r, deep, u=None, ready=False):
                        kts = range(4 * r, 4 * r + 4)
                        more, gmore = (0, 0) if u is None else (12, 4 * u)
                        if ready:
                            pe.wait_ge(ff_ready, FF_TILES * l + first + 4 * r + 4)
                        a_unit(i, ffT, kts, gd + 2 * c, r == 0, r == deep - 1, None, u, more, gmore)

                    if first == 0:
                        with pe.Fori(0, 2) as u:
                            for cc in range(2):
                                for r in range(6):
                                    down(d0 + 6 * cc + r, cc, r, 6, u, cc == 0)
                    else:
                        for c in range(CHUNKS):
                            for r in range(5):
                                if (c, r) != (CHUNKS - 1, 4):
                                    down(d0 + 5 * c + r, c, r, 5, None, c == 0)
                        last_unit(UNITS - 1, ffT, range(16, 20), gd + 6)


def _tiles_b(w, cols):
    k, n = w.shape
    return w.reshape(k // P, P, n // P, P).transpose(2, 1, 0, 3).reshape(n // P, P, -1)[:cols]


def _tiles_a(w, deep=4):
    k, n = w.shape
    return w.reshape(k // (P * deep), deep, P, n // CHUNK, CHUNK).transpose(3, 0, 2, 1, 4).reshape(-1, P, deep * CHUNK)


def _column(v):
    return v.reshape(-1, P).T


def kernel(**inputs):
    import concourse.bacc as _bacc
    from concourse.bass_utils import run_bass_kernel_spmd as _run

    a = {k: np.asarray(v) for k, v in inputs.items()}
    weights = np.zeros((DEPTH * UNITS, P, UNIT), np.float32)
    cols = np.zeros((DEPTH, P, COLS), np.float32)
    rows = np.zeros((DEPTH, P, 32), np.float32)
    Q, K, V, Z, XBC, DT = 0, 1024, 2048, 3072, 4096, 5632
    xbc_order = [8, 9, 10, 11, *range(8)]
    for l in range(DEPTH):
        w = weights[l * UNITS:(l + 1) * UNITS]
        w_in = a["w_in"][l]
        w[U_V:U_XBC] = _tiles_a(w_in[:, V:Z])
        w[U_XBC:U_Z] = _tiles_b(w_in[:, XBC:DT], 12)[xbc_order]
        w[U_Z:U_QK] = _tiles_b(w_in[:, Z:XBC], 8)
        q, k = _tiles_a(w_in[:, Q:K]), _tiles_a(w_in[:, K:V])
        for c in range(2):
            w[U_QK + 8 * c:U_QK + 8 * c + 4] = q[4 * c:4 * c + 4]
            w[U_QK + 8 * c + 4:U_QK + 8 * c + 8] = k[4 * c:4 * c + 4]
        w[U_WS:U_PA] = _tiles_a(a["w_out"][l][ATTN_WIDTH:])[[2 * c + part for c, part in WS_ORDER]]
        w[U_WA:U_PB] = _tiles_a(a["w_out"][l][:ATTN_WIDTH])
        gate, emb = _tiles_a(a["w_pe_gate"][l]), _tiles_a(a["w_pe_proj"][l], 2)
        w[U_GATE:U_UP1] = gate
        w[U_PA:U_WA, :, 0:2 * CHUNK] = emb[0:2]
        w[U_PB:U_GATE, :, 0:2 * CHUNK] = emb[2:4]
        up = _tiles_b(a["w_up"][l], 2 * FF_TILES).reshape(2, FF_TILES, P, UNIT).swapaxes(0, 1)
        w[U_UP1:U_DN1] = up[:FF1].reshape(-1, P, UNIT)
        w[U_UP2:U_DN2] = up[FF1:].reshape(-1, P, UNIT)
        w[U_DN1:U_UP2] = _tiles_a(a["w_down"][l][:FF1 * P])
        w[U_DN2:UNITS] = _tiles_a(a["w_down"][l][FF1 * P:])

        c = cols[l]
        conv_w = a["ssd_conv_w"][l].reshape(4, XBC_TILES, P)[:, xbc_order]
        c[:, C_XW:C_XB] = conv_w.transpose(2, 1, 0).reshape(P, -1)
        c[:, C_XB:C_SN] = _column(a["ssd_conv_b"][l])[:, xbc_order]
        c[:, C_SN:C_AN] = _column(a["ssd_norm_g"][l])
        c[:, C_AN:C_D] = _column(a["attn_norm_g"][l])
        c[:, C_D:C_L1G] = _column(np.repeat(a["ssd_d"][l], SSD_HD))
        c[:, C_L1G:C_L1B] = _column(a["ln1_g"][l])
        c[:, C_L1B:C_FW] = _column(a["ln1_b"][l])
        ffn_w = a["ffn_conv_w"][l].reshape(3, 2, FF_TILES, P)
        c[:, C_FW:C_FB] = ffn_w.transpose(3, 2, 1, 0).reshape(P, -1)
        c[:, C_FB:COLS] = a["ffn_conv_b"][l].reshape(2, FF_TILES, P).transpose(2, 1, 0).reshape(P, -1)
        rows[l, :, 0:16] = a["ssd_dt_bias"][l]
        rows[l, :, 16:32] = a["ssd_a_log"][l]

    consts = np.zeros((P, CONSTS), np.float32)
    i = np.arange(P)
    consts[:, K_ID:K_ID + P] = np.eye(P)
    consts[:, K_ONE:K_ONE + P] = 1.0
    consts[:, K_COL + 1] = 1.0
    consts[:, K_TRI:K_TRI + P] = i[:, None] <= i[None, :]
    hidden = np.float32(-3e38)
    query_key = np.where(i[None, :] <= i[:, None], np.float32(0), hidden)
    consts[:, K_AMASK:K_AMASK + P] = query_key
    consts[:, K_AMASK + 2 * P:K_AMASK + 3 * P] = query_key
    consts[:, K_SMASK:K_SMASK + P] = query_key.T
    consts[:, K_FREQ:K_FREQ + 16] = np.float32(1.0) / (np.float32(500000.0) ** (np.arange(0, 32, 2, dtype=np.float32)
                                                                                   / np.float32(32)))
    norm_rows = np.zeros((2 * DEPTH + 1, 2, D_MODEL), np.float32)
    norm_rows[0, 0] = 1.0
    for l in range(DEPTH):
        norm_rows[2 * l + 1] = a["ln1_g"][l], a["ln1_b"][l]
        norm_rows[2 * l + 2] = a["ln2_g"][l], a["ln2_b"][l]
    x = a["x"][0]
    arrays = {
        "x_tok": x.reshape(HALVES, P, D_MODEL).transpose(1, 0, 2),
        "p_T": a["p"][:, 0].transpose(0, 2, 1).reshape(DEPTH, 2, P, SEQ).transpose(0, 2, 1, 3),
        "pos": a["positions"].reshape(HALVES, P).T,
        "weights": weights,
        "w_dt": a["w_in"][:, :, DT:].reshape(DEPTH, KT, P, 16).transpose(0, 2, 1, 3),
        "cols": cols,
        "cols_in": norm_rows[2::2].reshape(DEPTH, 2 * KT, P).transpose(0, 2, 1),
        "rows": rows,
        "norm_rows": norm_rows,
        "consts": consts,
    }
    nc = _bacc.Bacc("TRN2", target_bir_lowering=False, num_devices=1)
    args = []
    for name, v in arrays.items():
        arrays[name] = v = np.ascontiguousarray(v)
        args.append(nc.dram_tensor(name, v.shape, mybir.dt.from_np(v.dtype), kind="ExternalInput").ap())
    out = nc.dram_tensor("out", (P, HALVES, D_MODEL), F32, kind="ExternalOutput").ap()
    build(nc, *args, out)
    r = _run(nc, [arrays], core_ids=[0])
    return r.results[0]["out"].transpose(1, 0, 2).reshape(1, SEQ, D_MODEL)
```
